# Optimizing a Trainium2 kernel written in Bass

```python
import math
import jax, jax.numpy as jnp
from jax import lax
import numpy as np

D_MODEL = 1024
BATCH = 1
SEQ = 512
DEPTH = 1

N_MEM = 256
HEAD_DIM = 64
SSD_HEADS = 6
SSD_WIDTH = SSD_HEADS * HEAD_DIM
SSD_GROUPS = 2
SSD_STATE = 64
SSD_CONV = 4
SSD_CHUNK = 128
SSD_CONV_CH = SSD_WIDTH + 2 * SSD_GROUPS * SSD_STATE
SB_HEADS = 6
SB_WIDTH = SB_HEADS * HEAD_DIM
SB_BLOCK = 128
MEM_HEADS = 4
MEM_WIDTH = MEM_HEADS * HEAD_DIM
D_MIX = SSD_WIDTH + SB_WIDTH + MEM_WIDTH
IN_SPLITS = [SSD_WIDTH, SSD_CONV_CH, SSD_HEADS, SB_WIDTH, SB_WIDTH, SB_WIDTH, MEM_WIDTH]
D_IN = sum(IN_SPLITS)
PEER_HEADS = 8
PEER_NKEYS = 128
PEER_EXPERTS = PEER_NKEYS * PEER_NKEYS
PEER_DKEY = 128
PEER_TOPK = 16
PEER_BLOCK = 128
EPS = 1e-6

kernel_name = "hymba_ssd_stickbreak_peer_trunk"

def rmsnorm(x, g):
    xf = x.astype(jnp.float32)
    y = xf * lax.rsqrt(jnp.mean(xf * xf, axis=-1, keepdims=True) + EPS)
    return (y * g.astype(jnp.float32)).astype(x.dtype)

def causal_depthwise_conv(x, w, b):
    k_w, ch = w.shape
    y = lax.conv_general_dilated(
        x, w.astype(x.dtype)[:, None, :], window_strides=(1,), padding=[(k_w - 1, 0)],
        dimension_numbers=("NWC", "WIO", "NWC"), feature_group_count=ch)
    return y + b.astype(x.dtype)

def ssd_scan(xh, dt, a, bm, cm):
    bsz, seqlen, nh, hp = xh.shape
    ns = bm.shape[-1]
    q = SSD_CHUNK
    nc = seqlen // q
    xdt = (xh * dt[..., None]).reshape(bsz, nc, q, nh, hp)
    adt = (dt * a).reshape(bsz, nc, q, nh)
    bm = bm.reshape(bsz, nc, q, nh, ns)
    cm = cm.reshape(bsz, nc, q, nh, ns)
    a_cs = jnp.cumsum(adt, axis=2)
    seg = a_cs[:, :, :, None, :] - a_cs[:, :, None, :, :]
    causal = jnp.tril(jnp.ones((q, q), dtype=bool))[None, None, :, :, None]
    lmat = jnp.exp(jnp.where(causal, seg, -jnp.inf))
    y_diag = jnp.einsum("bclhn,bcshn,bclsh,bcshp->bclhp", cm, bm, lmat, xdt)
    decay_s = jnp.exp(a_cs[:, :, -1:, :] - a_cs)
    states = jnp.einsum("bclhn,bclh,bclhp->bchpn", bm, decay_s, xdt)
    chunk_decay = jnp.exp(a_cs[:, :, -1, :])

    def step(h, inp):
        s_c, d_c = inp
        return h * d_c[:, :, None, None] + s_c, h

    h0 = jnp.zeros((bsz, nh, hp, ns), dtype=jnp.float32)
    _, h_in = lax.scan(step, h0, (jnp.swapaxes(states, 0, 1), jnp.swapaxes(chunk_decay, 0, 1)))
    h_in = jnp.swapaxes(h_in, 0, 1)
    y_off = jnp.einsum("bclhn,bchpn,bclh->bclhp", cm, h_in, jnp.exp(a_cs))
    return (y_diag + y_off).reshape(bsz, seqlen, nh, hp)

def ssd_mixer(u_z, u_xbc, u_dt, conv_w, conv_b, dt_bias, a_log, d_skip, norm_g):
    bsz, seqlen, _ = u_z.shape
    xbc = jax.nn.silu(causal_depthwise_conv(u_xbc, conv_w, conv_b))
    xs, bs, cs = jnp.split(xbc, [SSD_WIDTH, SSD_WIDTH + SSD_GROUPS * SSD_STATE], axis=-1)
    rep = SSD_HEADS // SSD_GROUPS
    xh = xs.reshape(bsz, seqlen, SSD_HEADS, HEAD_DIM).astype(jnp.float32)
    bm = jnp.repeat(bs.reshape(bsz, seqlen, SSD_GROUPS, SSD_STATE), rep, axis=2).astype(jnp.float32)
    cm = jnp.repeat(cs.reshape(bsz, seqlen, SSD_GROUPS, SSD_STATE), rep, axis=2).astype(jnp.float32)
    dt = jax.nn.softplus(u_dt.astype(jnp.float32) + dt_bias.astype(jnp.float32))
    a = -jnp.exp(a_log.astype(jnp.float32))
    y = ssd_scan(xh, dt, a, bm, cm) + xh * d_skip.astype(jnp.float32)[:, None]
    y = y.reshape(bsz, seqlen, SSD_WIDTH)
    return rmsnorm(y * jax.nn.silu(u_z.astype(jnp.float32)), norm_g)

def stick_breaking_attention(q, k, v):
    bsz, seqlen, nh, dh = q.shape
    q = jnp.transpose(q, (0, 2, 1, 3))
    k = jnp.transpose(k, (0, 2, 1, 3))
    v = jnp.transpose(v, (0, 2, 1, 3))
    scale = dh ** -0.5
    outs = []
    for i in range(seqlen // SB_BLOCK):
        start = i * SB_BLOCK
        end = start + SB_BLOCK
        qb = q[:, :, start:end]
        kp = k[:, :, :end]
        vp = v[:, :, :end]
        z = jnp.einsum("bhqd,bhkd->bhqk", qb, kp).astype(jnp.float32) * scale
        strict = jnp.arange(end)[None, :] < jnp.arange(start, end)[:, None]
        log_beta = jax.nn.log_sigmoid(z)
        log_keep = jnp.where(strict, jax.nn.log_sigmoid(-z), 0.0)
        suffix = lax.cumsum(log_keep, axis=3, reverse=True) - log_keep
        w = jnp.where(strict, jnp.exp(log_beta + suffix), 0.0)
        outs.append(jnp.einsum("bhqk,bhkd->bhqd", w.astype(vp.dtype), vp))
    out = jnp.concatenate(outs, axis=2)
    return jnp.transpose(out, (0, 2, 1, 3)).reshape(bsz, seqlen, nh * dh)

def memory_cross_attention(q, mk, mv, qg, kg):
    bsz, seqlen, nh, dh = q.shape
    q = rmsnorm(q, qg)
    mk = rmsnorm(mk, kg)
    s = jnp.einsum("bshd,bmhd->bhsm", q, mk).astype(jnp.float32) * (dh ** -0.5)
    p = jax.nn.softmax(s, axis=-1)
    o = jnp.einsum("bhsm,bmhd->bshd", p.astype(mv.dtype), mv)
    return o.reshape(bsz, seqlen, nh * dh)

def peer_ffn(h, wq, keys, u_tab, v_tab):
    bsz, seqlen, d = h.shape
    t = bsz * seqlen
    hf = h.reshape(t, d)
    q = (hf @ wq).reshape(t, PEER_HEADS, 2, PEER_DKEY // 2)
    scores = jnp.einsum("thcd,hcnd->thcn", q, keys).astype(jnp.float32)
    s_top, i_top = lax.top_k(scores, PEER_TOPK)
    cand = s_top[:, :, 0, :, None] + s_top[:, :, 1, None, :]
    cand_idx = i_top[:, :, 0, :, None] * PEER_NKEYS + i_top[:, :, 1, None, :]
    best, pos = lax.top_k(cand.reshape(t, PEER_HEADS, PEER_TOPK * PEER_TOPK), PEER_TOPK)
    eidx = jnp.take_along_axis(cand_idx.reshape(t, PEER_HEADS, PEER_TOPK * PEER_TOPK), pos, axis=-1)
    gates = jax.nn.softmax(best, axis=-1)

    def block(args):
        xb, ib, gb = args
        act = jax.nn.gelu(jnp.einsum("thkd,td->thk", u_tab[ib], xb).astype(jnp.float32), approximate=False)
        w = (gb * act).astype(xb.dtype)
        return jnp.einsum("thk,thkd->td", w, v_tab[ib])

    nb = t // PEER_BLOCK
    out = lax.map(block, (hf.reshape(nb, PEER_BLOCK, d),
                          eidx.reshape(nb, PEER_BLOCK, PEER_HEADS, PEER_TOPK),
                          gates.reshape(nb, PEER_BLOCK, PEER_HEADS, PEER_TOPK)))
    return out.reshape(bsz, seqlen, d)

def setup_inputs(seed: int = 0) -> dict:
    key = jax.random.key(seed)
    ks = jax.random.split(key, 24)
    f32 = jnp.float32
    L = DEPTH

    def nrm(k, shape, scale):
        return jax.random.normal(k, shape, dtype=f32) * scale

    def gain(k, shape):
        return 1.0 + 0.05 * jax.random.normal(k, shape, dtype=f32)

    dt0 = jnp.exp(jax.random.uniform(ks[5], (L, SSD_HEADS), dtype=f32,
                                     minval=math.log(1e-3), maxval=math.log(1e-1)))
    dt_bias = dt0 + jnp.log(-jnp.expm1(-dt0))
    a_log = jnp.log(jax.random.uniform(ks[6], (L, SSD_HEADS), dtype=f32, minval=1.0, maxval=16.0))
    return {
        "x": nrm(ks[0], (BATCH, SEQ, D_MODEL), 1.0),
        "mem": nrm(ks[1], (BATCH, N_MEM, D_MODEL), 1.0),
        "norm1_g": gain(ks[2], (L, D_MODEL)),
        "w_in": nrm(ks[3], (L, D_MODEL, D_IN), D_MODEL ** -0.5),
        "conv_w": nrm(ks[4], (L, SSD_CONV, SSD_CONV_CH), SSD_CONV ** -0.5),
        "conv_b": nrm(ks[7], (L, SSD_CONV_CH), 0.02),
        "dt_bias": dt_bias,
        "a_log": a_log,
        "d_skip": gain(ks[8], (L, SSD_HEADS)),
        "ssd_norm_g": gain(ks[9], (L, SSD_WIDTH)),
        "sb_out_g": gain(ks[10], (L, SB_WIDTH)),
        "mem_norm_g": gain(ks[11], (L, D_MODEL)),
        "w_mem_kv": nrm(ks[12], (L, D_MODEL, 2 * MEM_WIDTH), D_MODEL ** -0.5),
        "mq_norm_g": gain(ks[13], (L, HEAD_DIM)),
        "mk_norm_g": gain(ks[14], (L, HEAD_DIM)),
        "mem_out_g": gain(ks[15], (L, MEM_WIDTH)),
        "w_out": nrm(ks[16], (L, D_MIX, D_MODEL), D_MIX ** -0.5),
        "norm2_g": gain(ks[17], (L, D_MODEL)),
        "peer_wq": nrm(ks[18], (L, D_MODEL, PEER_HEADS * PEER_DKEY), D_MODEL ** -0.5),
        "peer_keys": nrm(ks[19], (L, PEER_HEADS, 2, PEER_NKEYS, PEER_DKEY // 2), (PEER_DKEY // 2) ** -0.5),
        "peer_u": nrm(ks[20], (L, PEER_EXPERTS, D_MODEL), D_MODEL ** -0.5),
        "peer_v": nrm(ks[21], (L, PEER_EXPERTS, D_MODEL), PEER_HEADS ** -0.5),
    }

def reference(x, mem, norm1_g, w_in, conv_w, conv_b, dt_bias, a_log, d_skip, ssd_norm_g,
              sb_out_g, mem_norm_g, w_mem_kv, mq_norm_g, mk_norm_g, mem_out_g, w_out,
              norm2_g, peer_wq, peer_keys, peer_u, peer_v):
    bsz, seqlen, _ = x.shape
    split_pts = list(np.cumsum(IN_SPLITS)[:-1])
    for l in range(DEPTH):
        h = rmsnorm(x, norm1_g[l])
        proj = h @ w_in[l]
        u_z, u_xbc, u_dt, q_sb, k_sb, v_sb, q_mem = jnp.split(proj, split_pts, axis=-1)

        y_ssd = ssd_mixer(u_z, u_xbc, u_dt, conv_w[l], conv_b[l], dt_bias[l], a_log[l],
                          d_skip[l], ssd_norm_g[l])

        hs = (bsz, seqlen, SB_HEADS, HEAD_DIM)
        y_sb = stick_breaking_attention(q_sb.reshape(hs), k_sb.reshape(hs), v_sb.reshape(hs))
        y_sb = rmsnorm(y_sb, sb_out_g[l])

        mem_kv = rmsnorm(mem, mem_norm_g[l]) @ w_mem_kv[l]
        mk, mv = jnp.split(mem_kv, 2, axis=-1)
        mhs = (bsz, N_MEM, MEM_HEADS, HEAD_DIM)
        y_mem = memory_cross_attention(q_mem.reshape(bsz, seqlen, MEM_HEADS, HEAD_DIM),
                                       mk.reshape(mhs), mv.reshape(mhs), mq_norm_g[l], mk_norm_g[l])
        y_mem = rmsnorm(y_mem, mem_out_g[l])

        y = jnp.concatenate([y_ssd.astype(x.dtype), y_sb.astype(x.dtype), y_mem.astype(x.dtype)], axis=-1) @ w_out[l]
        x = x + y.astype(x.dtype)

        h2 = rmsnorm(x, norm2_g[l])
        x = x + peer_ffn(h2, peer_wq[l], peer_keys[l], peer_u[l], peer_v[l]).astype(x.dtype)
    return x


_drawn_inputs = setup_inputs


def setup_inputs(seed=0):
    import zlib

    import numpy as np

    out = dict(_drawn_inputs(seed))
    spreads = {}
    factors = {'conv_b': 3.287}
    for name, (base, spread) in spreads.items():
        noise = np.random.default_rng([zlib.crc32(name.encode()), seed]).standard_normal(out[name].shape)
        drawn = base * np.exp(spread * noise) if base else spread * noise
        out[name] = __import__('jax').numpy.asarray(drawn.astype(out[name].dtype))
    for name, factor in factors.items():
        out[name] = (out[name] * factor).astype(out[name].dtype)
    return out
```

```python
from contextlib import ExitStack

import numpy as np
import concourse.bass as bass
from concourse import mybir

F32 = mybir.dt.float32
F32R = mybir.dt.float32r
U32 = mybir.dt.uint32
ALU = mybir.AluOpType
ACT = mybir.ActivationFunctionType
AX = mybir.AxisListType

P = 128
D = 1024
DC = D // P
T = 512
NT = T // P
M = 256
MT = M // P
HD = 64
SSD_H, SSD_G, CONV = 6, 2, 4
HPG = SSD_H // SSD_G
SSD_W = SSD_H * HD
CONV_CH = SSD_W + 2 * SSD_G * HD
SC, CC = SSD_W // P, CONV_CH // P
SB_H, SB_W = 6, 384
MEM_H, MEM_W = 4, 256
EPS = 1e-6
PH = 8
NK = 128
TOPK = 16
HK = PH * TOPK
NE = NK * NK
TG = P
TD = T - TG
DT = TD // P
NEG = -3.0e38

CHUNKS = ([("xbc", SSD_W + P * i) for i in range(CC)]
          + [("q", SSD_W + CONV_CH + SSD_H + P * i) for i in range(3)]
          + [("k", SSD_W + CONV_CH + SSD_H + SB_W + P * i) for i in range(3)]
          + [("v", SSD_W + CONV_CH + SSD_H + 2 * SB_W + P * i) for i in range(3)]
          + [("z", P * i) for i in range(3)]
          + [("qm", SSD_W + CONV_CH + SSD_H + 3 * SB_W + P * i) for i in range(2)]
          + [("mk", P * i) for i in range(2)] + [("mv", MEM_W + P * i) for i in range(2)])
CHUNK_OF = {}
for _n, (_kind, _) in enumerate(CHUNKS):
    CHUNK_OF.setdefault(_kind, _n)
LAST_USE = [{"v": f"v{NT - 1}", "mv": f"mv{MT - 1}"}.get(kind, f"{kind}{n - CHUNK_OF[kind]}")
            for n, (kind, _) in enumerate(CHUNKS)]
DT_COL = SSD_W + CONV_CH
RING = 8
R = [(0, 3), (3, 10), (12, 19), (21, 27)]
R_SCORES = [2, 6, 15, None]
R_SOFTMAX = [3, 7, 16, 24]
LAG = 4
H = [(10, 12), (19, 21), (27, 29)]
PASSES = NK // 4
PIECES = 16
R_GATHER = [None, 0, 44, 88]
H_GATHER = [28, 72, 112]
SB_AT = (0, 512, 1024, 896)
SB_N = 1280

JOBS = (["ssqx", "rowx"] + [f"xbc{i}" for i in range(5)] + ["dt"] + [f"q{i}" for i in range(3)]
        + [f"k{i}" for i in range(3)] + [f"v{i}" for i in range(NT)] + [f"z{i}" for i in range(3)]
        + [f"qm{i}" for i in range(2)] + ["ssqm", "rowm", "mk0", "mk1", "mv0", "mv1", "mkss0", "mkss1", "qmss"]
        + [f"{a}{t}" for t in range(NT) for a in ("tr", "cb", "dec", "segA", "segB", "ea", "st")
           if not (a == "ea" and t == 0) and not (a == "st" and t == NT - 1)]
        + ["y0", "y1", "y2", "ssqy"]
        + [x for c in range(2) for t in range(NT + 1)
           for x in ([f"sc{c}{t}"] if t < NT else []) + ([f"pT{c}{t - 1}"] if t else [])
           + ([f"ym{c}"] if t == NT else [])] + ["ssqym"])
JOB = {name: n for n, name in enumerate(JOBS)}


def trunk(nc, xT_d, x_d, memT_d, wch_d, wdt_d, par_d, dtb_d, alog_d, g2row_d, wout_d, wq_d, keys_d,
          uT_d, u_d, v_d, out_d):
    gates_d = nc.dram_tensor("gates_scratch", [NK, P, TD], F32).ap()
    acts_d = nc.dram_tensor("acts_scratch", [NK, P, TD], F32).ap()
    x1_d = nc.dram_tensor("x1_scratch", [P, NT, D], F32).ap()
    ctx = ExitStack()
    with ctx:
        def sem(name):
            return ctx.enter_context(nc.semaphore(name))

        def sb(name, shape, dt=F32, where=ctx):
            return where.enter_context(nc.sbuf_tensor(name, shape, dt))

        psum = ctx.enter_context(nc.psum_tensor("psum", [P, 8, 512], F32))

        ident, ones = sb("ident", [P, P]), sb("ones", [P, P])
        iota128 = sb("iota128", [P, P])
        iota16 = sb("iota16", [P, TOPK])
        eps = sb("eps", [P, 2])
        par = sb("par", [P, 64])
        rowr2, rq = sb("rowr2", [P, NT]), sb("rq", [P, 16])
        mstat = sb("mstat", [P, 4, 2 * NT, 2])
        h2T = sb("h2T", [P, DC, T])
        wring = sb("wring", [P, RING, DC, P])
        eidx = sb("eidx", [P, HK], U32)
        gate0 = sb("gate0", [P, HK])
        h2row = sb("h2row", [P, 2, D])
        xT = h2T
        g1p, gmp = par[:, 0:8], par[:, 8:16]
        convw, convb = par[:, 16:36], par[:, 36:41]
        dskip, ssdg, sbg = par[:, 41:44], par[:, 44:47], par[:, 47:50]
        memg, mqg, mkg = par[:, 50:52], par[:, 52:53], par[:, 53:54]

        first = ExitStack()
        x1 = sb("x1", [P, NT, D], where=first)
        upto = sb("upto", [P, P], where=first)
        after = sb("after", [P, P], where=first)
        from_on = sb("from_on", [P, P], where=first)
        halves = sb("halves", [P, P], where=first)
        one = ExitStack()
        xg = sb("xg", [P, DC, T], where=one)
        ymix = xg
        qT, kT = sb("qT", [P, 3, T], where=one), sb("kT", [P, 3, T], where=one)
        vrow = sb("vrow", [P, NT, SB_W], where=one)
        wdt = sb("wdt", [P, DC, SSD_H], where=one)
        dtb, alog = sb("dtb", [P, SSD_H], where=one), sb("alog", [P, SSD_H], where=one)
        rsB = sb("rsB", [P, T], where=one)
        rowr = sb("rowr", [P, 16], where=one)
        onea = ExitStack()
        memT = sb("memT", [P, DC, M], where=onea)
        rmB = sb("rmB", [P, M], where=onea)
        zT = sb("zT", [P, SC, T], where=onea)
        cin = sb("cin", [P, CC, T + CONV - 1], where=onea)
        xcT = sb("xcT", [P, CC, T], where=onea)
        sq = sb("sq", [P, 2, T], where=onea)
        qmT, qsq = sb("qmT", [P, 2, T], where=onea), sb("qsq", [P, 2, T], where=onea)
        mkT, mksq = sb("mkT", [P, 2, M], where=onea), sb("mksq", [P, 2, M], where=onea)
        mvrow = sb("mvrow", [P, MT, MEM_W], where=onea)
        xn = sb("xn", [P, NT, 4 * P], where=onea)
        dts = sb("dts", [P, 5, NT, SSD_H], where=onea)
        dec, wdd = sb("dec", [P, NT, 12], where=onea), sb("wdd", [P, SSD_H], where=onea)
        sega = sb("sega", [P, 2, SSD_H, P], where=onea)
        adtb = sb("adtb", [P, 2, SSD_H, HD], where=onea)
        cbm = sb("cbm", [P, SSD_G, P], where=onea)
        xdd = sb("xdd", [P, SSD_H, HD], where=onea)
        cdec = sb("cdec", [P, NT, HPG, P], where=onea)
        state = sb("state", [P, NT, HPG, HD], where=onea)
        yg = sb("yg", [P, SC, T], where=onea)
        pr = sb("pr", [P, 2, 2, M], where=onea)
        pT = h2row[:].rearrange("p a (b n) -> p a b n", b=2)
        gk = sb("gk", [P, 1], where=onea)
        lm = x1[:, 0:3, :].rearrange("p a b -> p (a b)").rearrange("p (t h l) -> p t h l", t=NT, h=SSD_H)
        onea.close()
        oneb = ExitStack()
        wout = sb("wout", [P, DC, D], where=oneb)
        zs = sb("zs", [P, 2, 1280], where=oneb)
        lk = sb("lk", [P, 2, 1280], where=oneb)
        nk = sb("nk", [P, 2, 1280], where=oneb)
        wt = sb("wt", [P, 2, 1280], where=oneb)
        ysb = sb("ysb", [P, SC, T], where=oneb)
        sqs = sb("sqs", [P, SC, T], where=oneb)
        rbB = sb("rbB", [P, T], where=oneb)
        g2row = sb("g2row", [P, D], where=oneb)
        oneb.close()
        one.close()
        first.close()

        uhi, ulo = sb("uhi", [P, 2, DC, P], F32R), sb("ulo", [P, 2, DC, P], F32R)
        hhi, hlo = sb("hhi", [P, DC, TD], F32R), sb("hlo", [P, DC, TD], F32R)
        uraw = h2T[:].rearrange("p c t -> p (c t)").rearrange("p (s c e) -> p s c e", s=4, c=DC)
        idx4 = sb("idx4", [P, 4], U32)
        dots, wrow = sb("dots", [P, HK]), sb("wrow", [P, HK])
        urow3 = sb("urow3", [P, 3, D])
        urow = [h2row[:, 1, :], urow3[:, 0, :], urow3[:, 1, :], urow3[:, 2, :]]
        act_s = sb("act_s", [P, 4, TD])
        zr = sb("zr", [P, 512], F32R)
        two = ExitStack()
        pqT = sb("pqT", [P, PH, T], where=two)
        keysT = sb("keysT", [P, PH, NK], where=two)
        sco = sb("sco", [P, PH, 2, NK], where=two)
        top = sb("top", [P, PH, 2, TOPK], where=two)
        itop = sb("itop", [P, PH, 2, TOPK], U32, where=two)
        itopf = sb("itopf", [P, PH, 2, TOPK], where=two)
        cand = sb("cand", [P, PH, TOPK, TOPK], where=two)
        pick = cand
        best = sb("best", [P, PH, TOPK], where=two)
        pos = sb("pos", [P, PH, TOPK], U32, where=two)
        posab = sb("posab", [P, 2, PH, TOPK], U32, where=two)
        posf = sb("posf", [P, 2, PH, TOPK], where=two)
        routed = sb("routed", [P, 3, HK], where=two)
        sm = sb("sm", [P, 4, PH, TOPK], where=two)
        rT = sb("rT", [P, 3, P], where=two)
        hotA = cand[:].rearrange("p h a b -> p (h a b)").rearrange("p (s t i) -> p s t i", s=2, i=P)
        hotB = sb("hotB", [P, 2, 8, P], where=two)
        stage = [wring[:].rearrange("p a b c -> p (a b c)").rearrange("p (i t) -> p i t", t=P),
                 sb("stage", [P, NK // 2, P], where=two)[:]]
        two.close()

        vraw = sb("vraw", [P, 4, D])
        vhi, vlo = sb("vhi", [P, 4, D], F32R), sb("vlo", [P, 4, D], F32R)
        aring, gring = sb("aring", [P, 4, TD]), sb("gring", [P, 4, TD])
        wf = sb("wf", [P, 4, TD])
        whi, wlo = sb("whi", [P, 4, TD], F32R), sb("wlo", [P, 4, TD], F32R)
        acc0 = sb("acc0", [P, D])
        x1b = h2T[:].rearrange("p c t -> p (c t)").rearrange("p (t d) -> p t d", d=D)

        class Signals(dict):

            def __missing__(self, name):
                self[name] = sem(name)
                return self[name]
        s = Signals()
        w_in = [sem(f"w_in{i}") for i in range(RING)]
        job_full = [sem(f"job_full{b}") for b in range(8)]
        job_free = [sem(f"job_free{b}") for b in range(8)]
        u_in = [sem(f"u_in{i}") for i in range(4)]
        v_in = [sem(f"v_in{i}") for i in range(4)]
        g_in = [sem(f"g_in{i}") for i in range(4)]
        a_in = [sem(f"a_in{i}") for i in range(4)]
        act_stored = [sem(f"act_stored{i}") for i in range(4)]
        urow_in = [sem(f"urow_in{i}") for i in range(4)]
        vrow_in = [sem(f"vrow_in{i}") for i in range(4)]

        def bank(name):
            return psum[:, JOB[name] % 8, :]

        def full(eng, name):
            eng.wait_ge(job_full[JOB[name] % 8], JOB[name] // 8 + 1)

        def free(ins, name):
            ins.then_inc(job_free[JOB[name] % 8], 1)

        def chain(eng, sm_):
            n = [0]

            def link(ins):
                ins.then_inc(sm_, 1)
                n[0] += 1
                eng.wait_ge(sm_, n[0])
            return link

        def freed(eng, name):
            eng.wait_ge(job_free[JOB[name] % 8], JOB[name] // 8 + 1)

        block = ctx.enter_context(nc.Block())

        @block.sync
        def _(sp):
            sp.dma_start(par[:], par_d).then_inc(s["par_in"], 16)
            sp.dma_start(xT[:, 0:4, :], xT_d[:, 0:4, :]).then_inc(s["xT_in0"], 16)
            sp.dma_start(xT[:, 4:8, :], xT_d[:, 4:8, :]).then_inc(s["xT_in1"], 16)
            for n in range(len(CHUNKS)):
                if n >= RING:
                    full(sp, LAST_USE[n - RING])
                sp.dma_start(wring[:, n % RING, :, :], wch_d[n]).then_inc(w_in[n % RING], 16)
                if n == 1:
                    sp.dma_start(wdt[:], wdt_d).then_inc(s["wdt_in"], 16)
                    sp.dma_start(dtb[:], dtb_d).then_inc(s["wdt_in"], 16)
                    sp.dma_start(alog[:], alog_d).then_inc(s["wdt_in"], 16)
                if n == 5:
                    sp.dma_start(memT[:], memT_d).then_inc(s["memT_in"], 16)
            for n in range(len(CHUNKS) - RING, len(CHUNKS)):
                full(sp, LAST_USE[n])
            sp.dma_start(wring[:].rearrange("p a b c -> p (a b c)").rearrange("p (c n) -> p c n", c=DC),
                         wq_d.rearrange("(c p) n -> p c n", p=P)).then_inc(s["wq_in"], 16)
            sp.wait_ge(s["ymix_ready"], 5)
            sp.dma_start(wout[:], wout_d.rearrange("(c p) n -> p c n", p=P)).then_inc(s["wout_in"], 16)
            sp.dma_start(x1[:], x_d.rearrange("(t p) d -> p t d", p=P)).then_inc(s["x_in"], 16)
            sp.dma_start(g2row[:], g2row_d).then_inc(s["g2_in"], 16)
            sp.wait_ge(s["h2row_ready"], NT)
            sp.dma_start(keysT[:], keys_d).then_inc(s["keys_in"], 16)
            sp.dma_start(x1_d, x1[:]).then_inc(s["x1_stored"], 16)
            for k in range(4):
                sp.sem_inc(act_stored[k], 16)
            sp.wait_ge(s["pq_full"], PH)
            sp.wait_ge(s["hlo_ready"], 1)

            def load_u(k, i):
                sp.dma_start(uraw[:, k], uT_d[i]).then_inc(u_in[k], 16)

            def store_act(k, i):
                sp.wait_ge(s["act_ready"], i + 3)
                sp.dma_start(acts_d[i], act_s[:, k, :]).then_inc(act_stored[k], 16)

            def store_gates(tt, piece, e):
                n = NK // PIECES
                at = piece - e * (PIECES // 2)
                sp.dma_start(gates_d[bass.ds(piece * n, n), :, tt * P:(tt + 1) * P].rearrange("i j t -> j i t"),
                             stage[e][:, bass.ds(at * n, n), :]).then_inc(s["gate_stored"], 16)

            def pass_u(q, stored=None):
                for k in range(4):
                    if stored:
                        tt, a, each, e = stored
                        for i in range(each):
                            store_gates(tt, 4 * each * q + (each * k + i - 4 * each * a), e)
                    if not (isinstance(q, int) and q == PASSES - 1):
                        sp.wait_ge(s["u_split"], 4 * q + (k + 1))
                        sp.sem_inc(s["slot_go"], 1)
                        load_u(k, 4 * q + (k + 4))
                    if not (isinstance(q, int) and q == 0 and k == 0):
                        store_act((k - 1) % 4, 4 * q + (k - 1))

            def load_v(k, i):
                sp.dma_start(vraw[:, k, :], v_d[i]).then_inc(v_in[k], 16)

            def load_w(k, i):
                sp.dma_start(gring[:, k, :], gates_d[i]).then_inc(g_in[k], 16)
                sp.dma_start(aring[:, k, :], acts_d[i]).then_inc(a_in[k], 16)
            for k in range(4):
                load_u(k, k)
            pass_u(0)
            with sp.Fori(1, H[0][1]) as q:
                pass_u(q)
            for tt in range(DT):
                sp.wait_ge(s["g_free"], 16 * (tt + 1) + 2)
                a = H[tt][1]
                each = 1 if tt < DT - 1 else 2
                half = PIECES // 8 // each
                for e in range(2):
                    with sp.Fori(a + half * e, a + half * (e + 1)) as q:
                        pass_u(q, (tt, a, each, e))
                a += 2 * half
                if tt == DT - 2:
                    with sp.Fori(a, R[NT - 1][1]) as q:
                        pass_u(q)
                    sp.wait_ge(s["routed_ready"], NT)
                    for k in range(4):
                        load_v(k, k)
                    a = R[NT - 1][1]
                if tt < DT - 1:
                    with sp.Fori(a, H[tt + 1][1]) as q:
                        pass_u(q)
            pass_u(PASSES - 1)
            store_act(3, NK - 1)
            for k in range(4):
                sp.wait_ge(act_stored[k], 16 * (PASSES + 1))
            sp.wait_ge(s["gate_stored"], 16 * PIECES * DT)
            for k in range(4):
                load_w(k, k)
            sp.wait_ge(s["u_split"], NK)
            sp.dma_start(x1b, x1_d).then_inc(s["x1b_in"], 16)
            with sp.Fori(0, PASSES - 1) as q:
                for k in range(4):
                    sp.wait_ge(s["v_split"], 4 * q + (k + 1))
                    sp.wait_ge(s["wf_ready"], 4 * q + (k + 1))
                    sp.sem_inc(s["slot_go"], 1)
                    load_v(k, 4 * q + (k + 4))
                    load_w(k, 4 * q + (k + 4))
            for tt in range(NT):
                sp.wait_ge(s["final_ready"], tt + 1)
                sp.dma_start(out_d[tt * P:(tt + 1) * P, :], x1b[:, tt, :]).then_inc(s["out_done"], 16)
            sp.wait_ge(s["out_done"], 16 * NT)

        @block.gpsimd
        def _(pool):
            link = chain(pool, s["pchain"])
            g = nc.gpsimd
            link(g.memset(ones[:], 1.0))
            link(g.memset(eps[:, 0:1], EPS))
            link(g.memset(eps[:, 1:2], HD * EPS))
            link(g.iota(iota128[:], [[1, P]], base=0, channel_multiplier=0, allow_small_or_imprecise_dtypes=True))
            link(g.iota(iota16[:], [[1, TOPK]], base=0, channel_multiplier=0, allow_small_or_imprecise_dtypes=True))
            link(g.affine_select(out=upto[:], in_=ones[:], compare_op=ALU.is_ge, fill=0.0, base=0,
                                 pattern=[[1, P]], channel_multiplier=-1))
            link(g.affine_select(out=after[:], in_=ones[:], compare_op=ALU.is_gt, fill=0.0, base=0,
                                 pattern=[[-1, P]], channel_multiplier=1))
            link(g.affine_select(out=from_on[:], in_=ones[:], compare_op=ALU.is_ge, fill=0.0, base=0,
                                 pattern=[[-1, P]], channel_multiplier=1))
            link(g.affine_select(out=ident[:], in_=ones[:], compare_op=ALU.is_equal, fill=0.0, base=0,
                                 pattern=[[-1, P]], channel_multiplier=1))
            link(g.memset(halves[:], 0.0))
            link(g.memset(halves[0:64, 0:64], 1.0))
            link(g.memset(halves[64:128, 64:128], 1.0))
            g.memset(cin[:, :, 0:CONV - 1], 0.0).then_inc(s["consts"], 1)
            pool.wait_ge(s["adt_ready"], 1)
            for t in range(NT):
                if t >= 2:
                    full(pool, f"segB{t - 2}")
                g.tensor_tensor(sega[:, t % 2], after[:].unsqueeze(1).broadcast_to([P, SSD_H, P]),
                                dts[:, 4, t, :].unsqueeze(2).broadcast_to([P, SSD_H, P]),
                                ALU.mult).then_inc(s["sega_ready"], 1)
                if t:
                    if t == 3:
                        full(pool, "ea1")
                    g.tensor_copy(adtb[:, t % 2], dts[:, 4, t, :].unsqueeze(2).broadcast_to(
                        [P, SSD_H, HD])).then_inc(s["adtb_ready"], 1)
            diag = SB_AT
            for h in range(SB_H + 1):
                if h < SB_H:
                    pool.wait_ge(s["nk_ready"], h + 1)
                    for a in diag:
                        v_ = nk[:, h % 2, a:a + P]
                        g.affine_select(out=v_, in_=v_, compare_op=ALU.is_gt, fill=0.0, base=0,
                                        pattern=[[1, P]], channel_multiplier=-1).then_inc(s["nkm_ready"], 1)
                if h:
                    pool.wait_ge(s["sb_w"], h)
                    for a in diag:
                        v_ = wt[:, (h - 1) % 2, a:a + P]
                        g.affine_select(out=v_, in_=v_, compare_op=ALU.is_gt, fill=0.0, base=0,
                                        pattern=[[1, P]], channel_multiplier=-1).then_inc(s["sb_wm"], 1)
            pool.wait_ge(s["hhi_ready"], 1)
            g.tensor_tensor(hlo[:], h2T[:, :, TG:T], hhi[:].bitcast(F32), ALU.subtract).then_inc(s["hlo_ready"], 1)

            def lower_u(k, i):
                pool.wait_ge(s["uhi_ready"], i + 1)
                g.tensor_tensor(ulo[:, k % 2], uraw[:, k], uhi[:, k % 2].bitcast(F32), ALU.subtract).then_inc(s["u_split"], 1)

            def gather(table, k, j, turn, row_in, used, first):
                if not first:
                    pool.wait_ge(row_in[k], 16 * turn)
                g.tensor_copy(idx4[:, k:k + 1], eidx[:, bass.ds(j, 1)]).then_inc(s["idx_ready"], 1)
                pool.wait_ge(s["idx_ready"], j + 1 + (0 if table is u_d else HK))
                if used is not None:
                    pool.wait_ge(s[used], j + (-3 if table is u_d else 1))
                    pool.sem_inc(s["row_go"], 1)
                g.indirect_dma_start(urow[k], None, table, bass.IndirectOffsetOnAxis(idx4[:, k:k + 1], 0)).then_inc(row_in[k], 16)

            def gather_u(k, j, turn):
                first = isinstance(j, int) and j < 4
                gather(u_d, k, j, turn, urow_in, None if first else "dot_ready", first)

            def pass_u(q, a, j0):
                for k in range(4):
                    lower_u(k, 4 * q + k)
                    if j0 is not None:
                        gather_u((j0 + k) % 4, 4 * q + (j0 - 4 * a + k), q + ((j0 + k) // 4 - a))

            def weigh(q, a, tt, n):
                pool.wait_ge(s["hotC_ready"], 8 * q + (16 * tt - 8 * a + n + 1))
                g.tensor_tensor(hotB[:, 0], hotB[:, 0],
                                rT[:, 2, bass.ds(64 * q + (8 * n - 64 * a), 8)].unsqueeze(2).broadcast_to([P, 8, P]),
                                ALU.mult).then_inc(s["hotB_even"], 1)
            for t in range(NT):
                a, b = R[t]
                if t == 1:
                    pool.wait_ge(s["eidx_ready"], 1)
                    pass_u(a, a, 0)
                    with pool.Fori(a + 1, b) as q:
                        pass_u(q, a, 0)
                else:
                    with pool.Fori(a, b) as q:
                        pass_u(q, a, R_GATHER[t])
                if t:
                    a, b = H[t - 1]
                    j0 = H_GATHER[t - 1]

                    def pass_h(q):
                        for k in range(4):
                            weigh(q, a, t - 1, 2 * k)
                            for n in (2 * k, 2 * k + 1):
                                gather_u((j0 + n) % 4, 8 * q + (j0 - 8 * a + n), 2 * q + ((j0 + n) // 4 - 2 * a))
                            lower_u(k, 4 * q + k)
                    pool.wait_ge(s["rT_ready"], t)
                    with pool.Fori(a, b) as q:
                        pass_h(q)
            with pool.Fori(H[-1][1], PASSES) as q:
                pass_u(q, 0, None)
            pool.wait_ge(s["dot_ready"], HK)
            pool.wait_ge(s["gate_stored"], 16 * PIECES * DT)

            def pass_v(q):
                for k in range(4):
                    i = 4 * q + k
                    gather(v_d.rearrange("i e d -> (i e) d"), k, i, q, vrow_in, "vrow_free", isinstance(q, int) and q == 0)
                    pool.wait_ge(a_in[k], 16 * q + 16)
                    pool.wait_ge(g_in[k], 16 * q + 16)
                    pool.wait_ge(s["w_ready"], i + 1)
                    g.tensor_tensor(wf[:, k, :], aring[:, k, :], gring[:, k, :], ALU.mult).then_inc(s["wf_ready"], 1)
            pass_v(0)
            with pool.Fori(1, PASSES) as q:
                pass_v(q)

        @block.tensor
        def _(pe):
            def mm(out, lhsT, rhs, start=True, stop=True):
                return nc.tensor.matmul(out, lhsT, rhs, start=start, stop=stop)

            def job(name):
                n = JOB[name]
                if n >= 8:
                    pe.wait_ge(job_free[n % 8], n // 8)
                return bank(name)

            other_rows = chain(pe, s["rows_done"])

            def done(ins, name):
                ins.then_inc(job_full[JOB[name] % 8], 1)

            def chunk(n):
                pe.wait_ge(w_in[n % RING], 16 * (n // RING + 1))
                return wring[:, n % RING, :, :]

            def squares(all_name, row_name, ready, width, tiles):
                a, b = job(all_name), job(row_name)
                for c in range(DC):
                    pe.wait_ge(s[ready], c + 1)
                    whole = mm(a[:, 0:width], ones[:], sq[:, c % 2, 0:width], c == 0, c == DC - 1)
                    for t in range(tiles):
                        last = nc.tensor.matmul(b[:, t:t + 1], sq[:, c % 2, t * P:(t + 1) * P], ones[:, 0:1],
                                                start=(c == 0 and t == 0), stop=(c == DC - 1), skip_group_check=True)
                    if c < DC - 1:
                        last.then_inc(s["sq_used"], 1)
                    else:
                        done(whole, all_name)
                        done(last, row_name)

            def channels(name, n, rhs, width):
                o, w = job(name), chunk(n)
                for c in range(DC):
                    last = mm(o[:, 0:width], w[:, c, :], rhs[:, c, :], c == 0, c == DC - 1)
                done(last, name)

            def tokens(name, t, n, count, lhs):
                o = job(name)
                for i in range(count):
                    chunk(n + i)
                a = n % RING
                for c in range(DC):
                    last = mm(o[:, 0:count * P], lhs[:, c, t * P:(t + 1) * P], wring[:, a:a + count, c, :],
                              c == 0, c == DC - 1)
                done(last, name)

            pe.wait_ge(s["consts"], 1)
            squares("ssqx", "rowx", "sqx_ready", T, NT)
            pe.wait_ge(s["xg_ready"], DC)
            for i in range(CC):
                channels(f"xbc{i}", CHUNK_OF["xbc"] + i, xg, T)
            o = job("dt")
            pe.wait_ge(s["wdt_in"], 48)
            for t in range(NT):
                for c in range(DC):
                    last = mm(o[:, SSD_H * t:SSD_H * (t + 1)], xg[:, c, t * P:(t + 1) * P], wdt[:, c, :],
                              c == 0, c == DC - 1)
            done(last, "dt")
            for kind in ("q", "k"):
                for i in range(3):
                    channels(f"{kind}{i}", CHUNK_OF[kind] + i, xg, T)
            for t in range(NT):
                tokens(f"v{t}", t, CHUNK_OF["v"], 3, xg)
            for kind, count in (("z", 3), ("qm", 2)):
                for i in range(count):
                    channels(f"{kind}{i}", CHUNK_OF[kind] + i, xg, T)
            squares("ssqm", "rowm", "sqm_ready", M, MT)
            pe.wait_ge(s["memg_ready"], DC)
            for i in range(2):
                channels(f"mk{i}", CHUNK_OF["mk"] + i, memT, M)
            for t in range(MT):
                tokens(f"mv{t}", t, CHUNK_OF["mv"], 2, memT)
            for i in range(2):
                o = job(f"mkss{i}")
                pe.wait_ge(s["mksq_ready"], i + 1)
                done(mm(o[:, 0:M], halves[:], mksq[:, i, :]), f"mkss{i}")
            o = job("qmss")
            pe.wait_ge(s["qsq_ready"], 2)
            for t in range(NT):
                for i in range(2):
                    last = mm(o[:, 4 * t + 2 * i:4 * t + 2 * i + 2], qsq[:, i, t * P:(t + 1) * P], halves[:, 0:P:HD])
            done(last, "qmss")

            pe.wait_ge(s["xc_ready"], CC)
            for t in range(NT):
                cols = slice(t * P, (t + 1) * P)
                o = job(f"tr{t}")
                for i in range(4):
                    last = nc.tensor.transpose(o[:, i * P:(i + 1) * P], xcT[:, i, cols], ident[:])
                done(last, f"tr{t}")
                o = job(f"cb{t}")
                for g in range(SSD_G):
                    rows_ = slice(HD * g, HD * (g + 1))
                    last = mm(o[:, g * P:(g + 1) * P], xcT[rows_, 3, cols], xcT[rows_, 4, cols])
                    if g == 0:
                        other_rows(last)
                done(last, f"cb{t}")
                o = job(f"dec{t}")
                if t == 0:
                    pe.wait_ge(s["adt_ready"], 1)
                mm(o[:, 0:SSD_H], after[:], dts[:, 4, t, :])
                done(mm(o[:, SSD_H:2 * SSD_H], ones[:], dts[:, 4, t, :]), f"dec{t}")
                pe.wait_ge(s["sega_ready"], t + 1)
                for half, name in enumerate((f"segA{t}", f"segB{t}")):
                    o = job(name)
                    for i in range(3):
                        last = mm(o[:, i * P:(i + 1) * P], sega[:, t % 2, 3 * half + i, :], upto[:])
                    done(last, name)
                if t:
                    o = job(f"ea{t}")
                    pe.wait_ge(s["adtb_ready"], t)
                    for g in range(SSD_G):
                        for i in range(HPG):
                            last = mm(o[HD * g:HD * (g + 1), i * P:(i + 1) * P], adtb[:, t % 2, HPG * g + i, :], upto[:])
                    done(last, f"ea{t}")
                if t < NT - 1:
                    o = job(f"st{t}")
                    pe.wait_ge(s["xdd_ready"], t + 1)
                    for g in range(SSD_G):
                        last = mm(o[HD * g:HD * (g + 1), 0:HPG * HD], xn[:, t, SSD_W + HD * g:SSD_W + HD * (g + 1)],
                                  xdd[:, HPG * g:HPG * (g + 1), :])
                    done(last, f"st{t}")
            pe.wait_ge(s["m_ready"], NT)
            pe.wait_ge(s["cdec_ready"], NT - 1)
            freed(pe, f"st{NT - 2}")
            for i in range(SC):
                o = job(f"y{i}")
                for e in range(2):
                    h = 2 * i + e
                    g, hh = h // HPG, h % HPG
                    for t in range(NT):
                        out = o[HD * e:HD * (e + 1), t * P:(t + 1) * P]
                        last = mm(out, xn[:, t, HD * h:HD * (h + 1)], lm[:, t, h, :], True, t == 0)
                        if t:
                            last = mm(out, state[HD * g:HD * (g + 1), t, hh, :],
                                      cdec[HD * g:HD * (g + 1), t, hh, :], False, True)
                    if h == HPG - 1:
                        other_rows(last)
                done(last, f"y{i}")
            o = job("ssqy")
            for i in range(SC):
                pe.wait_ge(s["sqy_ready"], i + 1)
                last = mm(o, ones[:], cin[:, i, 0:T], i == 0, i == SC - 1)
            done(last, "ssqy")

            pe.wait_ge(s["mkn_ready"], 2)
            freed(pe, f"mv{MT - 1}")
            for c in range(2):
                for t in range(NT + 1):
                    if t < NT:
                        o = job(f"sc{c}{t}")
                        for e in range(2):
                            r_ = slice(HD * e, HD * (e + 1))
                            last = mm(o[:, e * M:(e + 1) * M], qmT[r_, c, t * P:(t + 1) * P], mkT[r_, c, :])
                            if e == 0:
                                other_rows(last)
                        done(last, f"sc{c}{t}")
                    if t:
                        n = NT * c + t - 1
                        o = job(f"pT{c}{t - 1}")
                        pe.wait_ge(s["pn_ready"], n + 1)
                        for e in range(2):
                            for m in range(MT):
                                last = nc.tensor.transpose(o[:, (2 * e + m) * P:(2 * e + m + 1) * P],
                                                           pr[:, n % 2, e, m * P:(m + 1) * P], ident[:])
                        done(last, f"pT{c}{t - 1}")
                o = job(f"ym{c}")
                freed(pe, f"pT{c}{NT - 1}")
                for e in range(2):
                    for m in range(MT):
                        last = mm(o[HD * e:HD * (e + 1), :], mvrow[:, m, HD * (2 * c + e):HD * (2 * c + e + 1)],
                                  pT[:, e, m, :], m == 0, m == MT - 1)
                done(last, f"ym{c}")
            o = job("ssqym")
            for i in range(2):
                pe.wait_ge(s["sqym_ready"], i + 1)
                last = mm(o, ones[:], sq[:, i, :], i == 0, i == 1)
            done(last, "ssqym")

            for b in range(8):
                pe.wait_ge(job_free[b], len([n for n in range(len(JOBS)) if n % 8 == b]))
            zb = psum[:, 0:3, :].rearrange("p b n -> p (b n)")
            sbk = psum[:, 3:6, :].rearrange("p b n -> p (b n)")

            def scores(h):
                if h:
                    pe.wait_ge(s["z_read"], h)
                e, c = h % 2, h // 2
                for j in range(NT):
                    last = mm(zb[:, SB_AT[j]:SB_AT[j] + T - j * P], kT[HD * e:HD * (e + 1), c, j * P:(j + 1) * P],
                              qT[HD * e:HD * (e + 1), c, j * P:T])
                last.then_inc(s["z_full"], 1)

            def kept(h):
                pe.wait_ge(s["nkm_ready"], 4 * (h + 1))
                if h:
                    pe.wait_ge(s["arg_ready"], h)
                for j in range(NT):
                    for i in range(j, NT):
                        last = mm(sbk[:, SB_AT[j] + (i - j) * P:SB_AT[j] + T - j * P],
                                  (from_on if i == j else ones)[:], nk[:, h % 2, SB_AT[i]:SB_AT[i] + T - i * P],
                                  i == j, i == NT - 1)
                last.then_inc(s["kept_full"], 1)

            def values(h):
                pe.wait_ge(s["sb_wm"], 4 * (h + 1))
                e, c = h % 2, h // 2
                if c == 2 and e == 0:
                    pe.wait_ge(s["ysb_ready"], 1)
                for j in range(NT):
                    last = mm(psum[HD * e:HD * (e + 1), 6 + c % 2, j * P:T], vrow[:, j, HD * h:HD * (h + 1)],
                              wt[:, h % 2, SB_AT[j]:SB_AT[j] + T - j * P], j == 0, j == NT - 1)
                last.then_inc(s["av_full"], 1)
            scores(0)
            for h in range(SB_H):
                if h < SB_H - 1:
                    scores(h + 1)
                kept(h)
                if h:
                    values(h - 1)
            values(SB_H - 1)
            for i in range(SC):
                pe.wait_ge(s["sqs_ready"], i + 1)
                last = mm(psum[:, 0, :], ones[:], sqs[:, i, :], i == 0, i == SC - 1)
            last.then_inc(s["sbss_full"], 1)

            pe.wait_ge(s["ymix_ready"], 8)
            pe.wait_ge(s["wout_in"], 16)
            for t in range(NT + 1):
                if t < NT:
                    for half in range(2):
                        n = 2 * t + half
                        if n >= 4:
                            pe.wait_ge(s["x1_ready"], n - 3)
                        for c in range(DC):
                            last = mm(psum[:, 1 + n % 4, :], ymix[:, c, t * P:(t + 1) * P],
                                      wout[:, c, half * 512:(half + 1) * 512], c == 0, c == DC - 1)
                        last.then_inc(s["o_full"], 1)
                if t:
                    pe.wait_ge(s["h2row_ready"], t)
                    for half in range(2):
                        n = 2 * (t - 1) + half
                        if n >= 2:
                            pe.wait_ge(s["h2T_ready"], n - 1)
                        for i in range(4):
                            c = 4 * half + i
                            last = nc.tensor.transpose(psum[:, 5 + half, i * P:(i + 1) * P],
                                                       h2row[:, min(t - 1, 1), c * P:(c + 1) * P], ident[:])
                        last.then_inc(s["h2t_full"], 1)

            pe.wait_ge(s["wq_in"], 16)
            pe.wait_ge(s["h2T_ready"], 2 * NT)
            wq = wring[:].rearrange("p a b c -> p (a b c)").rearrange("p (c n) -> p c n", c=DC)
            for h in range(PH):
                pe.wait_ge(s["x1_ready"], 2 * NT)
                if h >= 4:
                    pe.wait_ge(s["pq_ready"], h - 3)
                for c in range(DC):
                    last = mm(psum[:, 1 + h % 4, :], wq[:, c, h * P:(h + 1) * P], h2T[:, c, :], c == 0, c == DC - 1)
                last.then_inc(s["pq_full"], 1)
            pe.wait_ge(s["keys_in"], 16)
            pe.wait_ge(s["pq_ready"], PH)

            def key_scores(t):
                if t == NT - 1:
                    pe.wait_ge(s["rT_ready"], 1)
                for i in range(PH // 2):
                    n = 4 * t + i
                    if n >= 2:
                        pe.wait_ge(s["sco_ready"], n - 1)
                    for c in range(2):
                        r_ = slice(HD * c, HD * (c + 1))
                        for h in (2 * i, 2 * i + 1):
                            a = (2 * (h % 2) + c) * P
                            last = mm(psum[:, 2 + n % 2, a:a + P], pqT[r_, h, t * P:(t + 1) * P], keysT[r_, h, :])
                        if c == 0:
                            other_rows(last)
                    last.then_inc(s["sco_full"], 1)

            def turned(tt):
                pe.wait_ge(s["routed_ready"], tt + 2)
                pe.wait_ge(s["sco_ready"], 4 * min(tt + 3, NT))
                if tt:
                    pe.wait_ge(s["rT_ready"], tt)
                for i in range(3):
                    last = nc.tensor.transpose(psum[:, 2, i * P:(i + 1) * P], routed[:, i, :], ident[:])
                last.then_inc(s["rT_full"], 1)

            def up(k, i):
                pe.wait_ge(s["uhi_ready"], i + 1)
                pe.wait_ge(s["act_ready"], i + 1)
                out = psum[:, k % 2, 0:TD]
                for c in range(DC):
                    mm(out, uhi[:, k % 2, c, :], hhi[:, c, :], c == 0, False)
                    mm(out, uhi[:, k % 2, c, :], hlo[:, c, :], False, False)
                pe.wait_ge(s["u_split"], i + 1)
                for c in range(DC):
                    last = mm(out, ulo[:, k % 2, c, :], hhi[:, c, :], False, c == DC - 1)
                last.then_inc(s["p1_done"], 1)

            def ups(a, b):
                with pe.Fori(a, b) as q:
                    for k in range(4):
                        up(k, 4 * q + k)

            def gates(q, a, tt, n):
                k = n % 2
                pe.wait_ge(s["hotA_ready"], 8 * q + (16 * tt - 8 * a + n + 1))
                pe.wait_ge(s["hotB_odd" if k else "hotB_even"], 4 * q + (8 * tt - 4 * a + n // 2 + 1))
                pe.wait_ge(s["g_free"], 8 * q + (16 * tt - 8 * a + n + 1))
                for i in range(8):
                    last = mm(psum[:, 4 + 2 * k + i // 4, (i % 4) * P:(i % 4 + 1) * P], hotB[:, k, i, :], hotA[:, k, i, :])
                last.then_inc(s["g_full"], 1)
            pe.sem_inc(s["g_full"], 2)
            pe.sem_inc(s["p1_done"], 2)
            key_scores(0)
            pe.wait_ge(s["hlo_ready"], 1)
            for t in range(NT):
                a, b = R[t]
                if t < NT - 1:
                    ups(a, R_SCORES[t])
                    key_scores(t + 1)
                    a = R_SCORES[t]
                if t:
                    ups(a, b - 1)
                    turned(t - 1)
                    a = b - 1
                ups(a, b)
                if t:
                    a, b = H[t - 1]
                    with pe.Fori(a, b) as q:
                        for k in range(4):
                            gates(q, a, t - 1, 2 * k)
                            gates(q, a, t - 1, 2 * k + 1)
                            up(k, 4 * q + k)
            pe.wait_ge(s["g_free"], 16 * DT + 2)
            pe.wait_ge(s["zero_ready"], 1)
            for b in range(2, 8):
                mm(psum[:, b, :], zr[:, 0:P], zr[:])
            pe.sem_inc(s["p2_done"], 4)
            ups(H[-1][1], PASSES)

            def down(k, i):
                pe.wait_ge(s["v_split"], i + 1)
                pe.wait_ge(s["w_ready"], i + 5)
                for t in range(DT):
                    for l_, r_ in ((whi, vhi), (whi, vlo), (wlo, vhi)):
                        for half in range(2):
                            last = nc.tensor.matmul(psum[:, 2 + 2 * t + half, :], l_[:, k, t * P:(t + 1) * P],
                                                    r_[:, k, half * 512:(half + 1) * 512], start=False, stop=True,
                                                    skip_group_check=True)
                last.then_inc(s["p2_done"], 1)
            with pe.Fori(0, PASSES) as q:
                for k in range(4):
                    down(k, 4 * q + k)

        @block.scalar
        def _(act):
            a_ = nc.scalar.activation
            link = chain(act, s["achain"])

            act.wait_ge(s["xT_in0"], 16)
            for c in range(DC):
                if c == 4:
                    act.wait_ge(s["xT_in1"], 16)
                if c >= 2:
                    act.wait_ge(s["sq_used"], c - 1)
                a_(sq[:, c % 2, :], xT[:, c, :], ACT.Square).then_inc(s["sqx_ready"], 1)
            act.wait_ge(s["consts"], 1)
            full(act, "ssqx")
            link(a_(rsB[:], bank("ssqx"), ACT.Ln, scale=1.0 / D, bias=eps[:, 0:1]))
            free(a_(rsB[:], rsB[:], ACT.Exp, scale=-0.5), "ssqx")
            full(act, "rowx")
            link(a_(rowr[:, 0:NT], bank("rowx")[:, 0:NT], ACT.Ln, scale=1.0 / D, bias=eps[:, 0:1]))
            free(a_(rowr[:, 0:NT], rowr[:, 0:NT], ACT.Exp, scale=-0.5), "rowx")
            act.wait_ge(s["wdt_in"], 48)
            a_(alog[:], alog[:], ACT.Exp).then_inc(s["dtp"], 1)
            act.wait_ge(s["udt"], 1)
            link(a_(dts[:, 2], dts[:, 1], ACT.Exp, scale=-1.0))
            a_(dts[:, 2], dts[:, 2], ACT.Ln, bias=1.0).then_inc(s["dtp"], 1)
            for i in range(CC):
                act.wait_ge(s["conv_ready"], i + 1)
                a_(xcT[:, i, :], xcT[:, i, :], ACT.Silu).then_inc(s["xc_ready"], 1)
            for t in range(NT):
                full(act, f"v{t}")
                free(a_(vrow[:, t, :], bank(f"v{t}")[:, 0:SB_W], ACT.Copy, scale=rowr[:, t:t + 1]), f"v{t}")
            for i in range(SC):
                freed(act, f"z{i}")
                a_(zT[:, i, :], zT[:, i, :], ACT.Silu).then_inc(s["silu_ready"], 1)
            act.wait_ge(s["memT_in"], 16)
            full(act, "rowx")
            for c in range(DC):
                if c >= 2:
                    act.wait_ge(s["sq_used"], DC - 1 + c - 1)
                a_(sq[:, c % 2, 0:M], memT[:, c, :], ACT.Square).then_inc(s["sqm_ready"], 1)
            full(act, "ssqm")
            link(a_(rmB[:], bank("ssqm")[:, 0:M], ACT.Ln, scale=1.0 / D, bias=eps[:, 0:1]))
            free(a_(rmB[:], rmB[:], ACT.Exp, scale=-0.5), "ssqm")
            full(act, "rowm")
            link(a_(rowr[:, 4:4 + MT], bank("rowm")[:, 0:MT], ACT.Ln, scale=1.0 / D, bias=eps[:, 0:1]))
            free(a_(rowr[:, 4:4 + MT], rowr[:, 4:4 + MT], ACT.Exp, scale=-0.5), "rowm")
            for i in range(2):
                freed(act, f"qm{i}")
                a_(qsq[:, i, :], qmT[:, i, :], ACT.Square).then_inc(s["qsq_ready"], 1)
            for i in range(2):
                freed(act, f"mk{i}")
                a_(mksq[:, i, :], mkT[:, i, :], ACT.Square).then_inc(s["mksq_ready"], 1)
            for t in range(MT):
                full(act, f"mv{t}")
                if t == 0:
                    freed(act, "rowm")
                free(a_(mvrow[:, t, :], bank(f"mv{t}")[:, 0:MEM_W], ACT.Copy, scale=rowr[:, 4 + t:5 + t]), f"mv{t}")
            for i in range(2):
                full(act, f"mkss{i}")
                link(a_(mksq[:, i, :], bank(f"mkss{i}")[:, 0:M], ACT.Ln, scale=1.0 / HD, bias=eps[:, 0:1]))
                free(a_(mksq[:, i, :], mksq[:, i, :], ACT.Exp, scale=-0.5), f"mkss{i}")
            full(act, "qmss")
            link(a_(rq[:], bank("qmss")[:, 0:16], ACT.Ln, bias=eps[:, 1:2]))
            free(a_(rq[:], rq[:], ACT.Exp, scale=-0.5), "qmss")

            for t in range(NT):
                full(act, f"tr{t}")
                free(a_(xn[:, t, :], bank(f"tr{t}"), ACT.Copy), f"tr{t}")
                full(act, f"dec{t}")
                free(a_(dec[:, t, :], bank(f"dec{t}")[:, 0:12], ACT.Exp), f"dec{t}")
                for half, name in enumerate((f"segA{t}", f"segB{t}")):
                    full(act, name)
                    free(a_(lm[:, t, 3 * half:3 * half + 3, :], bank(name)[:, 0:3 * P].rearrange("p (h l) -> p h l", h=3),
                            ACT.Exp), name)
                if t:
                    full(act, f"ea{t}")
                    free(a_(cdec[:, t], bank(f"ea{t}")[:, 0:3 * P].rearrange("p (h l) -> p h l", h=3), ACT.Exp), f"ea{t}")
            for i in range(SC):
                act.wait_ge(s["yg_ready"], i + 1)
                a_(cin[:, i, 0:T], yg[:, i, :], ACT.Square).then_inc(s["sqy_ready"], 1)
            full(act, "ssqy")
            link(a_(rsB[:], bank("ssqy"), ACT.Ln, scale=1.0 / SSD_W, bias=eps[:, 0:1]))
            free(a_(rsB[:], rsB[:], ACT.Exp, scale=-0.5), "ssqy")

            def turned(n):
                c, t = divmod(n, NT)
                full(act, f"pT{c}{t}")
                if n == NT:
                    full(act, "ym0")
                free(a_(pT[:, :, :, t * P:(t + 1) * P], bank(f"pT{c}{t}").rearrange("p (e m l) -> p e m l", e=2, m=2),
                        ACT.Copy), f"pT{c}{t}")
            for n in range(2 * NT):
                c, t = divmod(n, NT)
                act.wait_ge(s["smax_ready"], n + 1)
                if n >= 2:
                    c2, t2 = divmod(n - 2, NT)
                    full(act, f"pT{c2}{t2}")
                o = bank(f"sc{c}{t}")
                for e in range(2):
                    ins = a_(pr[:, n % 2, e, :], o[:, e * M:(e + 1) * M], ACT.Exp,
                             scale=rq[:, 4 * t + 2 * c + e:4 * t + 2 * c + e + 1], bias=mstat[:, 1, n, e:e + 1],
                             accum_out=mstat[:, 2, n, e:e + 1])
                    if e == 0:
                        link(ins)
                free(ins, f"sc{c}{t}")
                if t:
                    turned(n - 1)
                if t == NT - 1:
                    turned(n)
                    freed(act, f"ym{c}")
                    if c == 0:
                        full(act, "rowm")
                    a_(sq[:, c, :], ymix[:, 6 + c, :], ACT.Square).then_inc(s["sqym_ready"], 1)
            full(act, "ssqym")
            rB2 = xcT[:, 4, :]
            link(a_(rB2, bank("ssqym"), ACT.Ln, scale=1.0 / MEM_W, bias=eps[:, 0:1]))
            free(a_(rB2, rB2, ACT.Exp, scale=-0.5), "ssqym")

            act.wait_ge(s["ymix_ready"], 5)
            zb = psum[:, 0:3, :].rearrange("p b n -> p (b n)")[:, 0:SB_N]

            def front(h):
                k = h % 2
                act.wait_ge(s["z_full"], h + 1)
                if h >= 2:
                    act.wait_ge(s["arg_ready"], h - 1)
                a_(zs[:, k, :], zb, ACT.Copy, scale=HD ** -0.5).then_inc(s["zs_ready"], 1)
                ins = a_(lk[:, k, :], zb, ACT.Abs, scale=HD ** -0.5)
                ins.then_inc(s["z_read"], 1)
                act.wait_ge(s["z_read"], h + 1)
                link(a_(lk[:, k, :], lk[:, k, :], ACT.Exp, scale=-1.0))
                a_(lk[:, k, :], lk[:, k, :], ACT.Ln, bias=1.0).then_inc(s["lk_ready"], 1)
            front(0)
            for h in range(SB_H):
                if h < SB_H - 1:
                    front(h + 1)
                act.wait_ge(s["arg_ready"], h + 1)
                a_(wt[:, h % 2, :], wt[:, h % 2, :], ACT.Exp).then_inc(s["sb_w"], 1)
            for i in range(SC):
                act.wait_ge(s["ysb_ready"], i + 1)
                a_(sqs[:, i, :], ysb[:, i, :], ACT.Square).then_inc(s["sqs_ready"], 1)
            act.wait_ge(s["sbss_full"], 1)
            link(a_(rbB[:], psum[:, 0, :], ACT.Ln, scale=1.0 / SB_W, bias=eps[:, 0:1]))
            a_(rbB[:], rbB[:], ACT.Exp, scale=-0.5).then_inc(s["rbB_ready"], 1)

            def turned_rows(n):
                t, half = divmod(n, 2)
                act.wait_ge(s["h2t_full"], n + 1)
                a_(h2T[:, 4 * half:4 * half + 4, t * P:(t + 1) * P],
                   psum[:, 5 + half, :].rearrange("p (c l) -> p c l", c=4), ACT.Copy).then_inc(s["h2T_ready"], 1)
            for t in range(NT):
                act.wait_ge(s["x1_ready"], 2 * t + 2)
                if t >= 2:
                    act.wait_ge(s["h2t_full"], 2 * t)
                link(a_(h2row[:, min(t, 1), :], x1[:, t, :], ACT.Square, accum_out=rowr2[:, t:t + 1]))
                link(a_(rowr2[:, t:t + 1], rowr2[:, t:t + 1], ACT.Ln, scale=1.0 / D, bias=eps[:, 0:1]))
                a_(rowr2[:, t:t + 1], rowr2[:, t:t + 1], ACT.Exp, scale=-0.5).then_inc(s["r2_ready"], 1)
                if t:
                    turned_rows(2 * t - 2)
                    turned_rows(2 * t - 1)
            turned_rows(2 * NT - 2)
            turned_rows(2 * NT - 1)

            act.wait_ge(s["h2row_ready"], NT)
            for h in range(PH):
                act.wait_ge(s["pq_full"], h + 1)
                a_(pqT[:, h, :], psum[:, 1 + h % 4, :], ACT.Copy).then_inc(s["pq_ready"], 1)
            act.wait_ge(s["h2T_ready"], 2 * NT)
            a_(hhi[:], h2T[:, :, TG:T], ACT.Copy).then_inc(s["hhi_ready"], 1)
            act.sem_inc(s["g_free"], 2)
            act.sem_inc(s["act_ready"], 2)
            act.wait_ge(s["x1_stored"], 16)

            def key_scores(t):
                for i in range(PH // 2):
                    n = 4 * t + i
                    act.wait_ge(s["sco_full"], n + 1)
                    if t:
                        act.wait_ge(s["sco_used"], n - 3)
                    a_(sco[:, 2 * i:2 * i + 2, :, :], psum[:, 2 + n % 2, :].rearrange("p (h c n) -> p h c n", h=2, c=2),
                       ACT.Copy).then_inc(s["sco_ready"], 1)

            def softmax(t):
                act.wait_ge(s["soft_in"], t + 1)
                a_(sm[:, 1], sm[:, 0], ACT.Exp).then_inc(s["soft_out"], 1)

            def routed_turned(tt):
                act.wait_ge(s["rT_full"], tt + 1)
                if tt:
                    act.wait_ge(s["g_full"], 16 * tt + 2)
                a_(rT[:], psum[:, 2, 0:3 * P].rearrange("p (r l) -> p r l", r=3), ACT.Copy).then_inc(s["rT_ready"], 1)

            def upper_u(k, q):
                act.wait_ge(u_in[k], 16 * q + 16)
                act.wait_ge(s["p1_done"], 4 * q + (k + 1))
                a_(uhi[:, k % 2], uraw[:, k], ACT.Copy).then_inc(s["uhi_ready"], 1)

            def activations(k, q):
                before = (k - 1) % 4
                act.wait_ge(s["p1_done"], 4 * q + (k + 2))
                act.wait_ge(act_stored[before], 16 * q + (16 if k else 0))
                a_(act_s[:, before, :], psum[:, before % 2, 0:TD], ACT.Gelu).then_inc(s["act_ready"], 1)

            def tile(k, q):
                upper_u(k, q)
                if not (isinstance(q, int) and q == 0 and k == 0):
                    activations(k, q)

            def tiles(a, b):
                with act.Fori(a, b) as q:
                    for k in range(4):
                        tile(k, q)

            def weigh(q, a, tt, n):
                act.wait_ge(s["hotC_ready"], 8 * q + (16 * tt - 8 * a + n + 1))
                for i in range(8):
                    ins = a_(hotB[:, 1, i, :], hotB[:, 1, i, :], ACT.Copy, scale=rT[:, 2, bass.ds(64 * q + (8 * n + i - 64 * a), 1)])
                ins.then_inc(s["hotB_odd"], 1)

            def stage_gates(q, a, tt, n):
                k = n % 2
                act.wait_ge(s["g_full"], 8 * q + (16 * tt - 8 * a + n + 3))
                for e in range(2):
                    ins = a_(stage[e].rearrange("j i t -> j t i")[:, bass.ds(64 * q + (8 * n - 64 * a), 8), :],
                             psum[:, 4 + 2 * k:6 + 2 * k, :].rearrange("p b (t i) -> p (b t) i", t=4)[
                                 :, :, 64 * e:64 * (e + 1)], ACT.Copy)
                ins.then_inc(s["g_free"], 1)
            key_scores(0)
            for k in range(4):
                tile(k, 0)
            for t in range(NT):
                a, b = R[t]
                a = max(a, 1)
                if t < NT - 1:
                    tiles(a, R_SCORES[t])
                    key_scores(t + 1)
                    a = R_SCORES[t]
                tiles(a, R_SOFTMAX[t])
                softmax(t)
                if t:
                    tiles(R_SOFTMAX[t], b - 1)
                    routed_turned(t - 1)
                    tiles(b - 1, b)
                    if t >= 2:
                        act.wait_ge(s["gate_stored"], 16 * PIECES * (t - 1))
                    a, b = H[t - 1]
                    with act.Fori(a, b) as q:
                        for k in range(4):
                            upper_u(k, q)
                            weigh(q, a, t - 1, 2 * k + 1)
                            activations(k, q)
                            stage_gates(q, a, t - 1, 2 * k)
                            stage_gates(q, a, t - 1, 2 * k + 1)
            tiles(H[-1][1], PASSES)
            act.wait_ge(s["dot_ready"], HK)
            a_(wrow[:], dots[:], ACT.Gelu).then_inc(s["ge_ready"], 1)
            activations(0, PASSES)

            with act.Fori(0, PASSES) as q:
                for k in range(4):
                    act.wait_ge(v_in[k], 16 * q + 16)
                    act.wait_ge(s["p2_done"], 4 * q + (k + 1))
                    a_(vhi[:, k, :], vraw[:, k, :], ACT.Copy).then_inc(s["vhi_ready"], 1)
                    act.wait_ge(s["wf_ready"], 4 * q + (k + 1))
                    a_(whi[:, k, :], wf[:, k, :], ACT.Copy).then_inc(s["whi_ready"], 1)

        @block.vector
        def _(dve):
            v = nc.vector
            count = [0]

            def link(*several):
                for ins in several:
                    ins.then_inc(s["dchain"], 1)
                    count[0] += 1
                dve.wait_ge(s["dchain"], count[0])

            dve.wait_ge(s["par_in"], 16)
            for c in range(DC):
                dve.wait_ge(s["xT_in0" if c < 4 else "xT_in1"], 16)
                v.tensor_scalar(xg[:, c, :], xT[:, c, :], g1p[:, c:c + 1], None, ALU.mult).then_inc(s["xg_ready"], 1)
            dve.wait_ge(s["consts"], 1)
            freed(dve, "ssqx")
            for i in range(CC):
                full(dve, f"xbc{i}")
                free(v.tensor_tensor(cin[:, i, CONV - 1:], bank(f"xbc{i}"), rsB[:], ALU.mult), f"xbc{i}")
                freed(dve, f"xbc{i}")
                w = [convw[:, CONV * i + j:CONV * i + j + 1] for j in range(CONV)]
                link(v.tensor_scalar(xcT[:, i, :], cin[:, i, 0:T], w[0], convb[:, i:i + 1], ALU.mult, ALU.add))
                for j in range(1, CONV):
                    ins = v.scalar_tensor_tensor(xcT[:, i, :], cin[:, i, j:j + T], w[j], xcT[:, i, :], ALU.mult, ALU.add)
                    if j < CONV - 1:
                        link(ins)
                ins.then_inc(s["conv_ready"], 1)
            full(dve, "dt")
            freed(dve, "rowx")
            dve.wait_ge(s["wdt_in"], 48)
            free(v.tensor_tensor(dts[:, 0], bank("dt")[:, 0:NT * SSD_H].rearrange("p (t h) -> p t h", t=NT),
                                 rowr[:, 0:NT].unsqueeze(2).broadcast_to([P, NT, SSD_H]), ALU.mult), "dt")
            freed(dve, "dt")
            link(v.tensor_tensor(dts[:, 0], dts[:, 0], dtb[:].unsqueeze(1).broadcast_to([P, NT, SSD_H]), ALU.add))
            v.scalar_tensor_tensor(dts[:, 1], dts[:, 0], -1.0, dts[:, 0], ALU.mult, ALU.max).then_inc(s["udt"], 1)
            dve.wait_ge(s["dtp"], 2)
            link(v.scalar_tensor_tensor(dts[:, 3], dts[:, 0], 0.0, dts[:, 2], ALU.max, ALU.add))
            v.scalar_tensor_tensor(dts[:, 4], dts[:, 3], -1.0, alog[:].unsqueeze(1).broadcast_to([P, NT, SSD_H]),
                                   ALU.mult, ALU.mult).then_inc(s["adt_ready"], 1)
            for kind, dst in (("q", qT), ("k", kT), ("z", zT), ("qm", qmT)):
                for i in range(2 if kind == "qm" else 3):
                    full(dve, f"{kind}{i}")
                    free(v.tensor_tensor(dst[:, i, :], bank(f"{kind}{i}"), rsB[:], ALU.mult), f"{kind}{i}")
            link(v.tensor_tensor(gk[:], mqg, mkg, ALU.mult))
            for c in range(DC):
                dve.wait_ge(s["sqm_ready"], c + 1)
                v.tensor_scalar(memT[:, c, :], memT[:, c, :], gmp[:, c:c + 1], None, ALU.mult).then_inc(s["memg_ready"], 1)
            freed(dve, "ssqm")
            for i in range(2):
                full(dve, f"mk{i}")
                free(v.tensor_tensor(mkT[:, i, :], bank(f"mk{i}")[:, 0:M], rmB[:], ALU.mult), f"mk{i}")
            for i in range(2):
                freed(dve, f"mkss{i}")
                v.scalar_tensor_tensor(mkT[:, i, :], mkT[:, i, :], gk[:], mksq[:, i, :], ALU.mult,
                                       ALU.mult).then_inc(s["mkn_ready"], 1)

            for t in range(NT):
                cols = slice(t * P, (t + 1) * P)
                full(dve, f"cb{t}")
                free(v.tensor_tensor(cbm[:], bank(f"cb{t}")[:, 0:2 * P].rearrange("p (g l) -> p g l", g=2),
                                     upto[:].unsqueeze(1).broadcast_to([P, 2, P]), ALU.mult), f"cb{t}")
                freed(dve, f"cb{t}")
                freed(dve, f"dec{t}")
                if t < NT - 1:
                    link(v.tensor_tensor(wdd[:], dts[:, 3, t, :], dec[:, t, 0:SSD_H], ALU.mult))
                    freed(dve, f"tr{t}")
                    if t:
                        full(dve, f"st{t - 1}")
                    v.tensor_tensor(xdd[:], xn[:, t, 0:SSD_W].rearrange("p (h d) -> p h d", h=SSD_H),
                                    wdd[:].unsqueeze(2).broadcast_to([P, SSD_H, HD]), ALU.mult).then_inc(s["xdd_ready"], 1)
                freed(dve, f"segB{t}")
                freed(dve, f"segA{t}")
                for h in range(SSD_H):
                    ins = v.scalar_tensor_tensor(lm[:, t, h, :], lm[:, t, h, :], dts[:, 3, t, h:h + 1],
                                                 cbm[:, h // HPG, :], ALU.mult, ALU.mult)
                ins.then_inc(s["m_ready"], 1)
                dve.wait_ge(s["m_ready"], t + 1)
                if t:
                    freed(dve, f"ea{t}")
                    v.tensor_tensor(cdec[:, t], cdec[:, t], xcT[:, 4, cols].unsqueeze(1).broadcast_to([P, HPG, P]),
                                    ALU.mult).then_inc(s["cdec_ready"], 1)
                if t < NT - 1:
                    full(dve, f"st{t}")
                    if t == 0:
                        ins = v.tensor_copy(state[:, 1], bank("st0")[:, 0:HPG * HD].rearrange("p (h d) -> p h d", h=HPG))
                    else:
                        freed(dve, f"st{t - 1}")
                        for g in range(SSD_G):
                            r_ = slice(HD * g, HD * (g + 1))
                            for i in range(HPG):
                                a = SSD_H + HPG * g + i
                                ins = v.scalar_tensor_tensor(state[r_, t + 1, i, :], state[r_, t, i, :], dec[r_, t, a:a + 1],
                                                             bank(f"st{t}")[r_, i * HD:(i + 1) * HD], ALU.mult, ALU.add)
                    free(ins, f"st{t}")
            for i in range(SC):
                full(dve, f"y{i}")
                free(v.scalar_tensor_tensor(yg[:, i, :], xcT[:, i, :], dskip[:, i:i + 1], bank(f"y{i}"), ALU.mult, ALU.add),
                     f"y{i}")
                freed(dve, f"y{i}")
                dve.wait_ge(s["silu_ready"], i + 1)
                v.tensor_tensor(yg[:, i, :], yg[:, i, :], zT[:, i, :], ALU.mult).then_inc(s["yg_ready"], 1)
            freed(dve, "ssqy")
            for i in range(SC):
                v.scalar_tensor_tensor(ymix[:, i, :], yg[:, i, :], ssdg[:, i:i + 1], rsB[:], ALU.mult,
                                       ALU.mult).then_inc(s["ymix_ready"], 1)

            freed(dve, "qmss")

            def normalized(n):
                c, t = divmod(n, NT)
                freed(dve, f"sc{c}{t}")
                link(v.reciprocal(mstat[:, 3, n, :], mstat[:, 2, n, :]))
                for e in range(2):
                    ins = v.tensor_scalar(pr[:, n % 2, e, :], pr[:, n % 2, e, :], mstat[:, 3, n, e:e + 1], None, ALU.mult)
                ins.then_inc(s["pn_ready"], 1)
            for n in range(2 * NT):
                c, t = divmod(n, NT)
                full(dve, f"sc{c}{t}")
                link(v.tensor_reduce(mstat[:, 0, n, :], bank(f"sc{c}{t}").rearrange("p (e m) -> p e m", e=2), AX.X, ALU.max))
                v.scalar_tensor_tensor(mstat[:, 1, n, :], mstat[:, 0, n, :], -1.0, rq[:, 4 * t + 2 * c:4 * t + 2 * c + 2],
                                       ALU.mult, ALU.mult).then_inc(s["smax_ready"], 1)
                if t:
                    normalized(n - 1)
                if t == NT - 1:
                    normalized(n)
                    full(dve, f"ym{c}")
                    free(v.tensor_copy(ymix[:, 6 + c, :], bank(f"ym{c}")), f"ym{c}")
            freed(dve, "ssqym")
            freed(dve, "ym1")
            for c in range(2):
                v.scalar_tensor_tensor(ymix[:, 6 + c, :], ymix[:, 6 + c, :], memg[:, c:c + 1], xcT[:, 4, :], ALU.mult,
                                       ALU.mult).then_inc(s["ymix_ready"], 1)

            sbk = psum[:, 3:6, :].rearrange("p b n -> p (b n)")[:, 0:SB_N]
            dve.wait_ge(s["ymix_ready"], 5)

            def not_kept(h):
                dve.wait_ge(s["zs_ready"], h + 1)
                dve.wait_ge(s["lk_ready"], h + 1)
                if h >= 2:
                    dve.wait_ge(s["kept_full"], h - 1)
                v.scalar_tensor_tensor(nk[:, h % 2, :], zs[:, h % 2, :], 0.0, lk[:, h % 2, :], ALU.max,
                                       ALU.add).then_inc(s["nk_ready"], 1)

            def head_pair(c):
                dve.wait_ge(s["av_full"], 2 * c + 2)
                v.tensor_copy(ysb[:, c, :], psum[:, 6 + c % 2, :]).then_inc(s["ysb_ready"], 1)
            not_kept(0)
            for h in range(SB_H):
                if h < SB_H - 1:
                    not_kept(h + 1)
                dve.wait_ge(s["kept_full"], h + 1)
                if h >= 2:
                    dve.wait_ge(s["av_full"], h - 1)
                v.tensor_tensor(wt[:, h % 2, :], zs[:, h % 2, :], sbk, ALU.subtract).then_inc(s["arg_ready"], 1)
                if h in (3, 5):
                    head_pair(h // 2 - 1)
            head_pair(2)
            dve.wait_ge(s["rbB_ready"], 1)
            for i in range(SC):
                v.scalar_tensor_tensor(ymix[:, 3 + i, :], ysb[:, i, :], sbg[:, i:i + 1], rbB[:], ALU.mult,
                                       ALU.mult).then_inc(s["ymix_ready"], 1)

            dve.wait_ge(s["x_in"], 16)
            dve.wait_ge(s["g2_in"], 16)
            for t in range(NT + 1):
                if t < NT:
                    for half in range(2):
                        n = 2 * t + half
                        dve.wait_ge(s["o_full"], n + 1)
                        cols = slice(half * 512, (half + 1) * 512)
                        v.tensor_tensor(x1[:, t, cols], psum[:, 1 + n % 4, :], x1[:, t, cols], ALU.add).then_inc(s["x1_ready"], 1)
                if t:
                    dve.wait_ge(s["r2_ready"], t)
                    v.scalar_tensor_tensor(h2row[:, min(t - 1, 1), :], x1[:, t - 1, :], rowr2[:, t - 1:t], g2row[:], ALU.mult,
                                           ALU.mult).then_inc(s["h2row_ready"], 1)

            dotted = [0]

            def dot(j, k, turn):
                dve.wait_ge(urow_in[k], 16 * turn)
                v.scalar_tensor_tensor(urow[k], urow[k], 1.0, h2row[:, 0, :], ALU.mult, ALU.mult,
                                       accum_out=dots[:, bass.ds(j, 1)]).then_inc(s["dot_ready"], 1)

            def some_dots(t, part, of):
                if t:
                    start = max(R_GATHER[t] - LAG, 0)
                    early = 4 * (R_SOFTMAX[t] - R[t][0]) - 2
                    late = H_GATHER[t - 1] - LAG - start - early
                    goal = early * part // of if part <= of else early + late * (part - of) // of
                    while dotted[0] < start + goal:
                        dot(dotted[0], dotted[0] % 4, dotted[0] // 4 + 1)
                        dotted[0] += 1

            def top16(pairs):
                link(*[v.max(val[:, 0:8], row) for row, val, at in pairs])
                link(*[v.max_index(at[:, 0:8], val[:, 0:8], row) for row, val, at in pairs])
                link(*[v.match_replace(row, val[:, 0:8], row, NEG) for row, val, at in pairs])
                link(*[v.max(val[:, 8:16], row) for row, val, at in pairs])
                link(*[v.max_index(at[:, 8:16], val[:, 8:16], row) for row, val, at in pairs])

            def route(t):
                for i in range(PH // 2):
                    dve.wait_ge(s["sco_ready"], 4 * t + i + 1)
                    top16([(sco[:, h, c, :], top[:, h, c, :], itop[:, h, c, :]) for h in (2 * i, 2 * i + 1) for c in range(2)])
                    v.tensor_copy(itopf[:, 2 * i:2 * i + 2], itop[:, 2 * i:2 * i + 2]).then_inc(s["sco_used"], 1)
                    some_dots(t, i + 1, 6)
                if t >= 2:
                    dve.wait_ge(s["g_full"], 16 * (t - 1) + 2)
                link(v.tensor_tensor(cand[:], top[:, :, 0, :].unsqueeze(3).broadcast_to([P, PH, TOPK, TOPK]),
                                     top[:, :, 1, :].unsqueeze(2).broadcast_to([P, PH, TOPK, TOPK]), ALU.add))
                for i in range(0, PH, 4):
                    top16([(cand[:, h].rearrange("p a b -> p (a b)"), best[:, h, :], pos[:, h, :]) for h in range(i, i + 4)])
                    some_dots(t, 5 + i // 4, 6)
                v.tensor_tensor(sm[:, 0], best[:], best[:, :, 0:1].broadcast_to([P, PH, TOPK]),
                                ALU.subtract).then_inc(s["soft_in"], 1)
                link(v.tensor_scalar(posab[:, 0], pos[:], 4, None, ALU.logical_shift_right),
                     v.tensor_scalar(posab[:, 1], pos[:], 15, None, ALU.bitwise_and))
                link(v.tensor_copy(posf[:], posab[:]))
                dve.wait_ge(s["sco_used"], 4 * t + 4)
                if t >= 2:
                    dve.wait_ge(s["rT_full"], t - 1)
                for c in range(2):
                    link(v.tensor_tensor(pick[:], posf[:, c].unsqueeze(3).broadcast_to([P, PH, TOPK, TOPK]),
                                         iota16[:].unsqueeze(1).unsqueeze(1).broadcast_to([P, PH, TOPK, TOPK]), ALU.is_equal))
                    link(v.tensor_tensor(pick[:], pick[:], itopf[:, :, c, :].unsqueeze(2).broadcast_to([P, PH, TOPK, TOPK]),
                                         ALU.mult))
                    link(v.tensor_reduce(routed[:, c, :].rearrange("p (h k) -> p h k", h=PH), pick[:], AX.X, ALU.add))
                    if c == 0:
                        some_dots(t, 3, 2)
                dve.wait_ge(s["soft_out"], t + 1)
                link(v.tensor_reduce(sm[:, 2, :, 0:1].rearrange("p h o -> p (h o)"), sm[:, 1], AX.X, ALU.add))
                link(v.reciprocal(sm[:, 3, :, 0:1], sm[:, 2, :, 0:1]))
                v.tensor_tensor(routed[:, 2, :].rearrange("p (h k) -> p h k", h=PH), sm[:, 1],
                                sm[:, 3, :, 0:1].broadcast_to([P, PH, TOPK]), ALU.mult).then_inc(s["routed_ready"], 1)
                if t == 0:
                    dve.wait_ge(s["routed_ready"], 1)
                    v.tensor_copy(gate0[:], routed[:, 2, :])
                    link(v.scalar_tensor_tensor(eidx[:], routed[:, 0, :], float(NK), routed[:, 1, :], ALU.mult, ALU.add))
                    dve.sem_inc(s["eidx_ready"], 1)
                some_dots(t, 4, 2)

            def hot(tt):
                a, b = H[tt]
                j0 = H_GATHER[tt] - LAG
                dve.wait_ge(s["rT_ready"], tt + 1)
                with dve.Fori(a, b) as q:
                    for n in range(8):
                        k = n % 2
                        dve.wait_ge(s["g_full"], 8 * q + (16 * tt - 8 * a + n + 1))
                        for c, hot_, ready in ((1, hotB, "hotC_ready"), (0, hotA, "hotA_ready")):
                            v.tensor_tensor(hot_[:, k], iota128[:].unsqueeze(1).broadcast_to([P, 8, P]),
                                            rT[:, c, bass.ds(64 * q + (8 * n - 64 * a), 8)].unsqueeze(2).broadcast_to([P, 8, P]),
                                            ALU.is_equal).then_inc(s[ready], 1)
                        dot(8 * q + (j0 - 8 * a + n), n % 4, 2 * q + (j0 // 4 - 2 * a + n // 4 + 1))
                dotted[0] = j0 + 8 * (b - a)
            route(0)
            for t in range(1, NT):
                route(t)
                hot(t - 1)
            v.memset(zr[:].bitcast(F32), 0.0).then_inc(s["zero_ready"], 1)
            for j in range(HK - LAG, HK):
                dot(j, j % 4, j // 4 + 1)

            dve.wait_ge(s["gate_stored"], 16 * PIECES * DT)
            dve.sem_inc(s["w_ready"], 4)
            v.memset(acc0[:], 0.0).then_inc(s["vrow_free"], 4)
            dve.wait_ge(s["ge_ready"], 1)
            link(v.tensor_tensor(wrow[:], wrow[:], gate0[:], ALU.mult))
            with dve.Fori(0, PASSES) as q:
                for k in range(4):
                    i = 4 * q + k
                    dve.wait_ge(s["vhi_ready"], i + 1)
                    v.tensor_tensor(vlo[:, k, :], vraw[:, k, :], vhi[:, k, :].bitcast(F32), ALU.subtract).then_inc(s["v_split"], 1)
                    dve.wait_ge(s["whi_ready"], i + 1)
                    v.tensor_tensor(wlo[:, k, :], wf[:, k, :], whi[:, k, :].bitcast(F32), ALU.subtract).then_inc(s["w_ready"], 1)
                    dve.wait_ge(vrow_in[k], 16 * q + 16)
                    dve.wait_ge(s["vrow_free"], i + 4)
                    v.scalar_tensor_tensor(acc0[:], urow[k], wrow[:, bass.ds(i, 1)], acc0[:], ALU.mult,
                                           ALU.add).then_inc(s["vrow_free"], 1)
            dve.wait_ge(s["vrow_free"], NK + 4)
            dve.wait_ge(s["x1b_in"], 16)
            v.tensor_tensor(x1b[:, 0, :], x1b[:, 0, :], acc0[:], ALU.add).then_inc(s["final_ready"], 1)
            dve.wait_ge(s["p2_done"], NK + 4)
            for t in range(1, NT):
                for half in range(2):
                    cols = slice(half * 512, (half + 1) * 512)
                    ins = v.tensor_tensor(x1b[:, t, cols], psum[:, 2 * t + half, :], x1b[:, t, cols], ALU.add)
                ins.then_inc(s["final_ready"], 1)


_NAMES = ["xT", "x", "memT", "chunks", "wdt", "par", "dtb", "alog", "g2row", "wout", "wq", "keys", "uT", "u", "v"]


def kernel(x, mem, norm1_g, w_in, conv_w, conv_b, dt_bias, a_log, d_skip, ssd_norm_g, sb_out_g, mem_norm_g,
           w_mem_kv, mq_norm_g, mk_norm_g, mem_out_g, w_out, norm2_g, peer_wq, peer_keys, peer_u, peer_v):
    import concourse.bacc as bacc
    from concourse.bass_utils import run_bass_kernel_spmd

    def blocks(a):
        return a.reshape(DC, P, -1).transpose(1, 0, 2)

    def by_channel(a):
        return a.reshape(-1, P).T

    f = lambda a: np.asarray(a)[0]
    win, wkv = f(w_in), f(w_mem_kv)
    pad = np.zeros((P, 64 - 54), np.float32)
    data = {
        "xT": blocks(f(x).T), "x": f(x), "memT": blocks(f(mem).T),
        "chunks": np.stack([blocks((wkv if kind in ("mk", "mv") else win)[:, a:a + P]) for kind, a in CHUNKS]),
        "wdt": blocks(win[:, DT_COL:DT_COL + SSD_H]),
        "par": np.concatenate([
            by_channel(f(norm1_g)), by_channel(f(mem_norm_g)),
            f(conv_w).reshape(CONV, CC, P).transpose(2, 1, 0).reshape(P, CC * CONV), by_channel(f(conv_b)),
            by_channel(np.repeat(f(d_skip), HD)), by_channel(f(ssd_norm_g)), by_channel(f(sb_out_g)),
            by_channel(f(mem_out_g)), by_channel(np.tile(f(mq_norm_g), 2)), by_channel(np.tile(f(mk_norm_g), 2)), pad], axis=1),
        "dtb": np.broadcast_to(f(dt_bias), (P, SSD_H)), "alog": np.broadcast_to(f(a_log), (P, SSD_H)),
        "g2row": np.broadcast_to(f(norm2_g), (P, D)),
        "wout": f(w_out), "wq": f(peer_wq),
        "keys": f(peer_keys).transpose(1, 3, 0, 2).reshape(P, PH, NK),
        "uT": f(peer_u).reshape(NK, P, DC, P).transpose(0, 3, 2, 1), "u": f(peer_u), "v": f(peer_v).reshape(NK, P, D),
    }
    nc = bacc.Bacc("TRN2", target_bir_lowering=False, num_devices=1)
    arrays, args = {}, []
    for name in _NAMES:
        a = np.ascontiguousarray(data[name])
        arrays[f"in_{name}"] = a
        args.append(nc.dram_tensor(f"in_{name}", a.shape, mybir.dt.from_np(a.dtype), kind="ExternalInput").ap())
    args.append(nc.dram_tensor("out_0", (T, D), F32, kind="ExternalOutput").ap())
    trunk(nc, *args)
    r = run_bass_kernel_spmd(nc, [arrays], core_ids=[0])
    return r.results[0]["out_0"].reshape(1, T, D)
```

```python
from contextlib import ExitStack

import numpy as np
import concourse.bass as bass
from concourse import mybir

F32 = mybir.dt.float32
F32R = mybir.dt.float32r
U32 = mybir.dt.uint32
ALU = mybir.AluOpType
ACT = mybir.ActivationFunctionType
AX = mybir.AxisListType

P = 128
D = 1024
DC = D // P
T = 512
NT = T // P
M = 256
MT = M // P
HD = 64
SSD_H, SSD_G, CONV = 6, 2, 4
HPG = SSD_H // SSD_G
SSD_W = SSD_H * HD
CONV_CH = SSD_W + 2 * SSD_G * HD
SC, CC = SSD_W // P, CONV_CH // P
SB_H, SB_W = 6, 384
MEM_H, MEM_W = 4, 256
EPS = 1e-6
PH = 8
NK = 128
TOPK = 16
HK = PH * TOPK
NE = NK * NK
TG = P
TD = T - TG
DT = TD // P
NEG = -3.0e38

CHUNKS = ([("xbc", SSD_W + P * i) for i in range(CC)]
          + [("q", SSD_W + CONV_CH + SSD_H + P * i) for i in range(3)]
          + [("k", SSD_W + CONV_CH + SSD_H + SB_W + P * i) for i in range(3)]
          + [("v", SSD_W + CONV_CH + SSD_H + 2 * SB_W + P * i) for i in range(3)]
          + [("z", P * i) for i in range(3)]
          + [("qm", SSD_W + CONV_CH + SSD_H + 3 * SB_W + P * i) for i in range(2)]
          + [("mk", P * i) for i in range(2)] + [("mv", MEM_W + P * i) for i in range(2)])
CHUNK_OF = {}
for _n, (_kind, _) in enumerate(CHUNKS):
    CHUNK_OF.setdefault(_kind, _n)
LAST_USE = [{"v": f"v{NT - 1}", "mv": f"mv{MT - 1}"}.get(kind, f"{kind}{n - CHUNK_OF[kind]}")
            for n, (kind, _) in enumerate(CHUNKS)]
DT_COL = SSD_W + CONV_CH
SPLIT = [n for n, (kind, _) in enumerate(CHUNKS) if n >= 2 and kind in ("xbc", "q", "k", "z", "qm")]
RING = 8
R = [(0, 2), (2, 9), (11, 18), (20, 26)]
R_SCORES = [0, 5, 14, None]
R_SOFTMAX = [1, 7, 16, 24]
LAG = 4
H = [(9, 11), (18, 20), (26, 28)]
PASSES = NK // 4
LAST_U = [0, 3, 8, 13, 20, PASSES]
PIECES = 16
R_GATHER = [None, 0, 44, 88]
H_GATHER = [28, 72, 112]
SB_AT = (0, 512, 1024, 896)
SB_N = 1280

STEPS = [("ssd", 0, 0), ("mem", 0, 0), ("mem", 0, 1), ("ssd", 0, 1), ("mem", 0, 2), ("mem", 0, 3), ("mem", 0, 4),
         ("ssd", 0, 2), ("mem", 1, 0), ("mem", 1, 1), ("ssd", 0, 3), ("mem", 1, 2), ("mem", 1, 3), ("mem", 1, 4)]


def turned_at(t):
    return [t - 2] if 2 <= t < NT else [NT - 2, NT - 1] if t == NT else []


def step_jobs(kind, c, t):
    if kind == "ssd":
        return [f"{a}{t}" for a in ("tr", "cb", "dec", "segA", "segB", "ea", "st")
                if not (a == "ea" and t == 0) and not (a == "st" and t == NT - 1)]
    return ([f"sc{c}{t}"] if t < NT else []) + [f"pT{c}{u}" for u in turned_at(t)] + ([f"ym{c}"] if t == NT else [])


JOBS = (["xbc0", "xbc1", "ssqx", "xbc2", "rowx", "xbc3", "xbc4", "dt"] + [f"q{i}" for i in range(3)]
        + [f"k{i}" for i in range(3)] + [f"v{i}" for i in range(NT)] + [f"z{i}" for i in range(3)]
        + [f"qm{i}" for i in range(2)] + ["ssqm", "mk0", "mk1", "rowm", "mv0", "mv1", "mkss0", "mkss1", "qmss"]
        + [name for kind, c, t in STEPS for name in step_jobs(kind, c, t)]
        + ["y0", "y1", "y2", "ssqy", "ssqym"])
JOB = {name: n for n, name in enumerate(JOBS)}


def trunk(nc, xT_d, x_d, memT_d, wch_d, wdt_d, par_d, dtb_d, alog_d, g2row_d, wout_d, wq_d, keys_d,
          uT_d, u_d, v_d, out_d):
    gates_d = nc.dram_tensor("gates_scratch", [NK, P, TD], F32).ap()
    acts_d = nc.dram_tensor("acts_scratch", [NK, P, TD], F32).ap()
    x1_d = nc.dram_tensor("x1_scratch", [P, NT, D], F32).ap()
    ctx = ExitStack()
    with ctx:
        def sem(name):
            return ctx.enter_context(nc.semaphore(name))

        def sb(name, shape, dt=F32, where=ctx):
            return where.enter_context(nc.sbuf_tensor(name, shape, dt))

        psum = ctx.enter_context(nc.psum_tensor("psum", [P, 8, 512], F32))

        ident, ones = sb("ident", [P, P]), sb("ones", [P, P])
        iota128 = sb("iota128", [P, P])
        iota16 = sb("iota16", [P, TOPK])
        eps = sb("eps", [P, 2])
        par = sb("par", [P, 64])
        rowr2, rq = sb("rowr2", [P, NT]), sb("rq", [P, 16])
        mstat = sb("mstat", [P, 4, 2 * NT, 2])
        h2T = sb("h2T", [P, DC, T])
        wring = sb("wring", [P, RING, DC, P])
        eidx = sb("eidx", [P, HK], U32)
        gate0 = sb("gate0", [P, HK])
        blocks_hi = ExitStack()
        bhi = sb("bhi", [P, 2, DC, P], F32R, where=blocks_hi)
        blocks_hi.close()
        h2row = sb("h2row", [P, 2, D])
        xT = h2T
        g1p, gmp = par[:, 0:8], par[:, 8:16]
        convw, convb = par[:, 16:36], par[:, 36:41]
        dskip, ssdg, sbg = par[:, 41:44], par[:, 44:47], par[:, 47:50]
        memg, mqg, mkg = par[:, 50:52], par[:, 52:53], par[:, 53:54]

        first = ExitStack()
        xparts = ExitStack()
        xhi = sb("xhi", [P, DC, T], F32R, where=xparts)
        xparts.close()
        x1 = sb("x1", [P, NT, D], where=first)
        upto = sb("upto", [P, P], where=first)
        after = sb("after", [P, P], where=first)
        from_on = sb("from_on", [P, P], where=first)
        halves = sb("halves", [P, P], where=first)
        one = ExitStack()
        xg = sb("xg", [P, DC, T], where=one)
        ymix = xg
        qT, kT = sb("qT", [P, 3, T], where=one), sb("kT", [P, 3, T], where=one)
        vrow = sb("vrow", [P, NT, SB_W], where=one)
        wdt = sb("wdt", [P, DC, SSD_H], where=one)
        dtb, alog = sb("dtb", [P, SSD_H], where=one), sb("alog", [P, SSD_H], where=one)
        rsB = sb("rsB", [P, T], where=one)
        rowr = sb("rowr", [P, 16], where=one)
        onea = ExitStack()
        memT = sb("memT", [P, DC, M], where=onea)
        rmB = sb("rmB", [P, M], where=onea)
        zT = sb("zT", [P, SC, T], where=onea)
        cin = sb("cin", [P, CC, T + CONV - 1], where=onea)
        xcT = sb("xcT", [P, CC, T], where=onea)
        sq = sb("sq", [P, 2, T], where=onea)
        qmT, qsq = sb("qmT", [P, 2, T], where=onea), sb("qsq", [P, 2, T], where=onea)
        mkT, mksq = sb("mkT", [P, 2, M], where=onea), sb("mksq", [P, 2, M], where=onea)
        mvrow = sb("mvrow", [P, MT, MEM_W], where=onea)
        dts = sb("dts", [P, 5, NT, SSD_H], where=onea)
        gk = sb("gk", [P, 1], where=onea)
        lower = ExitStack()
        xlo, blo = sb("xlo", [P, DC, T], F32R, where=lower), sb("blo", [P, 2, DC, P], F32R, where=lower)
        lower.close()
        xn = sb("xn", [P, NT, 4 * P], where=onea)
        dec, wdd = sb("dec", [P, NT, 12], where=onea), sb("wdd", [P, SSD_H], where=onea)
        sega = sb("sega", [P, 2, SSD_H, P], where=onea)
        adtb = sb("adtb", [P, 2, SSD_H, HD], where=onea)
        cbm = sb("cbm", [P, SSD_G, P], where=onea)
        xdd = sb("xdd", [P, SSD_H, HD], where=onea)
        cdec = sb("cdec", [P, NT, HPG, P], where=onea)
        state = sb("state", [P, NT, HPG, HD], where=onea)
        yg = sb("yg", [P, SC, T], where=onea)
        pr = sb("pr", [P, 3, 2, M], where=onea)
        pT = h2row[:].rearrange("p a (b n) -> p a b n", b=2)
        lm = x1[:, 0:3, :].rearrange("p a b -> p (a b)").rearrange("p (t h l) -> p t h l", t=NT, h=SSD_H)
        onea.close()
        oneb = ExitStack()
        wout = sb("wout", [P, DC, D], where=oneb)
        zs = sb("zs", [P, 2, 1280], where=oneb)
        lk = sb("lk", [P, 2, 1280], where=oneb)
        nk = sb("nk", [P, 2, 1280], where=oneb)
        wt = sb("wt", [P, 2, 1280], where=oneb)
        ysb = sb("ysb", [P, SC, T], where=oneb)
        sqs = sb("sqs", [P, SC, T], where=oneb)
        rbB = sb("rbB", [P, T], where=oneb)
        g2row = sb("g2row", [P, D], where=oneb)
        oneb.close()
        one.close()
        first.close()

        uhi, ulo = sb("uhi", [P, 2, DC, P], F32R), sb("ulo", [P, 2, DC, P], F32R)
        hhi, hlo = sb("hhi", [P, DC, TD], F32R), sb("hlo", [P, DC, TD], F32R)
        uraw = h2T[:].rearrange("p c t -> p (c t)").rearrange("p (s c e) -> p s c e", s=4, c=DC)
        idx4 = sb("idx4", [P, 4], U32)
        dots, wrow = sb("dots", [P, HK]), sb("wrow", [P, HK])
        urow3 = sb("urow3", [P, 3, D])
        urow = [h2row[:, 1, :], urow3[:, 0, :], urow3[:, 1, :], urow3[:, 2, :]]
        act_s = sb("act_s", [P, 4, TD])
        zr = sb("zr", [P, 512], F32R)
        two = ExitStack()
        pqT = sb("pqT", [P, PH, T], where=two)
        keysT = sb("keysT", [P, PH, NK], where=two)
        sco = sb("sco", [P, PH, 2, NK], where=two)
        top = sb("top", [P, PH, 2, TOPK], where=two)
        itop = sb("itop", [P, PH, 2, TOPK], U32, where=two)
        itopf = sb("itopf", [P, PH, 2, TOPK], where=two)
        cand = sb("cand", [P, PH, TOPK, TOPK], where=two)
        pick = cand
        best = sb("best", [P, PH, TOPK], where=two)
        pos = sb("pos", [P, PH, TOPK], U32, where=two)
        posab = sb("posab", [P, 2, PH, TOPK], U32, where=two)
        posf = sb("posf", [P, 2, PH, TOPK], where=two)
        routed = sb("routed", [P, 3, HK], where=two)
        sm = sb("sm", [P, 4, PH, TOPK], where=two)
        rT = sb("rT", [P, 3, P], where=two)
        hotA = cand[:].rearrange("p h a b -> p (h a b)").rearrange("p (s t i) -> p s t i", s=2, i=P)
        hotB = sb("hotB", [P, 2, 8, P], where=two)
        parts = ExitStack()
        wqhi, wqlo = sb("wqhi", [P, 2, DC, P], F32R, where=parts), sb("wqlo", [P, 2, DC, P], F32R, where=parts)
        parts.close()
        stage = [wring[:].rearrange("p a b c -> p (a b c)").rearrange("p (i t) -> p i t", t=P),
                 sb("stage", [P, NK // 2, P], where=two)[:]]
        two.close()

        vraw = sb("vraw", [P, 4, D])
        vhi, vlo = sb("vhi", [P, 4, D], F32R), sb("vlo", [P, 4, D], F32R)
        aring, gring = sb("aring", [P, 4, TD]), sb("gring", [P, 4, TD])
        wf = sb("wf", [P, 4, TD])
        whi, wlo = sb("whi", [P, 4, TD], F32R), sb("wlo", [P, 4, TD], F32R)
        acc0 = sb("acc0", [P, D])
        x1b = h2T[:].rearrange("p c t -> p (c t)").rearrange("p (t d) -> p t d", d=D)

        class Signals(dict):

            def __missing__(self, name):
                self[name] = sem(name)
                return self[name]
        s = Signals()
        w_in = [sem(f"w_in{i}") for i in range(RING)]
        job_full = [sem(f"job_full{b}") for b in range(8)]
        job_free = [sem(f"job_free{b}") for b in range(8)]
        u_in = [sem(f"u_in{i}") for i in range(4)]
        v_in = [sem(f"v_in{i}") for i in range(4)]
        g_in = [sem(f"g_in{i}") for i in range(4)]
        a_in = [sem(f"a_in{i}") for i in range(4)]
        act_stored = [sem(f"act_stored{i}") for i in range(4)]
        row_in = [sem(f"row_in{i}") for i in range(4)]

        def bank(name):
            return psum[:, JOB[name] % 8, :]

        def full(eng, name):
            eng.wait_ge(job_full[JOB[name] % 8], JOB[name] // 8 + 1)

        def free(ins, name):
            ins.then_inc(job_free[JOB[name] % 8], 1)

        def chain(eng, sm_):
            n = [0]

            def link(ins):
                ins.then_inc(sm_, 1)
                n[0] += 1
                eng.wait_ge(sm_, n[0])
            return link

        def freed(eng, name):
            eng.wait_ge(job_free[JOB[name] % 8], JOB[name] // 8 + 1)

        block = ctx.enter_context(nc.Block())

        @block.sync
        def _(sp):
            sp.dma_start(par[:], par_d).then_inc(s["par_in"], 16)
            sp.dma_start(xT[:, 0:2, :], xT_d[:, 0:2, :]).then_inc(s["xT_in0"], 16)
            sp.dma_start(wring[:, 0, :, :], wch_d[0]).then_inc(w_in[0], 16)
            sp.dma_start(xT[:, 2:8, :], xT_d[:, 2:8, :]).then_inc(s["xT_in1"], 16)
            for n in range(1, len(CHUNKS)):
                if n >= RING:
                    full(sp, LAST_USE[n - RING])
                sp.dma_start(wring[:, n % RING, :, :], wch_d[n]).then_inc(w_in[n % RING], 16)
                if n == 1:
                    sp.dma_start(wdt[:], wdt_d).then_inc(s["wdt_in"], 16)
                    sp.dma_start(dtb[:], dtb_d).then_inc(s["wdt_in"], 16)
                    sp.dma_start(alog[:], alog_d).then_inc(s["wdt_in"], 16)
                if n == 5:
                    sp.dma_start(memT[:], memT_d).then_inc(s["memT_in"], 16)
            for n in range(len(CHUNKS) - RING, len(CHUNKS)):
                full(sp, LAST_USE[n])
            sp.dma_start(wring[:].rearrange("p a b c -> p (a b c)").rearrange("p (c n) -> p c n", c=DC),
                         wq_d.rearrange("(c p) n -> p c n", p=P)).then_inc(s["wq_in"], 16)
            sp.wait_ge(s["ymix_ready"], 5)
            sp.dma_start(wout[:], wout_d.rearrange("(c p) n -> p c n", p=P)).then_inc(s["wout_in"], 16)
            sp.dma_start(x1[:], x_d.rearrange("(t p) d -> p t d", p=P)).then_inc(s["x_in"], 16)
            sp.dma_start(g2row[:], g2row_d).then_inc(s["g2_in"], 16)
            sp.wait_ge(s["h2row_ready"], NT)
            sp.dma_start(keysT[:], keys_d).then_inc(s["keys_in"], 16)
            sp.dma_start(x1_d, x1[:]).then_inc(s["x1_stored"], 16)
            for k in range(4):
                sp.sem_inc(act_stored[k], 16)
            sp.wait_ge(s["pq_full"], 2)
            sp.wait_ge(s["hlo_ready"], 1)

            def load_u(k, i):
                sp.dma_start(uraw[:, k], uT_d[i]).then_inc(u_in[k], 16)

            def store_act(k, i):
                sp.wait_ge(s["act_ready"], i + 3)
                sp.dma_start(acts_d[i], act_s[:, k, :]).then_inc(act_stored[k], 16)

            def store_gates(tt, piece, e):
                n = NK // PIECES
                at = piece - e * (PIECES // 2)
                sp.dma_start(gates_d[bass.ds(piece * n, n), :, tt * P:(tt + 1) * P].rearrange("i j t -> j i t"),
                             stage[e][:, bass.ds(at * n, n), :]).then_inc(s["gate_stored"], 16)

            def pass_u(q, stored=None):
                for k in range(4):
                    if stored:
                        tt, a, each, e = stored
                        for i in range(each):
                            store_gates(tt, 4 * each * q + (each * k + i - 4 * each * a), e)
                    if not (isinstance(q, int) and q == PASSES - 1):
                        sp.wait_ge(s["u_split"], 4 * q + (k + 1))
                        sp.sem_inc(s["slot_go"], 1)
                        load_u(k, 4 * q + (k + 4))
                    if not (isinstance(q, int) and q == 0 and k == 0):
                        store_act((k - 1) % 4, 4 * q + (k - 1))

            def load_v(k, i):
                sp.dma_start(vraw[:, k, :], v_d[i]).then_inc(v_in[k], 16)

            def load_w(k, i):
                sp.dma_start(gring[:, k, :], gates_d[i]).then_inc(g_in[k], 16)
                sp.dma_start(aring[:, k, :], acts_d[i]).then_inc(a_in[k], 16)
            for k in range(4):
                load_u(k, k)
            pass_u(0)
            with sp.Fori(1, H[0][1]) as q:
                pass_u(q)
            for tt in range(DT):
                sp.wait_ge(s["g_free"], 16 * (tt + 1) + 2)
                a = H[tt][1]
                each = 1 if tt < DT - 1 else 2
                half = PIECES // 8 // each
                for e in range(2):
                    with sp.Fori(a + half * e, a + half * (e + 1)) as q:
                        pass_u(q, (tt, a, each, e))
                a += 2 * half
                if tt == DT - 2:
                    with sp.Fori(a, R[NT - 1][1]) as q:
                        pass_u(q)
                    sp.wait_ge(s["routed_ready"], NT)
                    for k in range(4):
                        load_v(k, k)
                    a = R[NT - 1][1]
                if tt < DT - 1:
                    with sp.Fori(a, H[tt + 1][1]) as q:
                        pass_u(q)
            sp.wait_ge(s["gate_stored"], 16 * PIECES * DT)
            for k in range(4):
                sp.wait_ge(act_stored[k], 32)
                load_w(k, k)
            pass_u(PASSES - 2)
            store_act(3, NK - 5)
            for n, (a, b) in enumerate(zip(LAST_U, LAST_U[1:])):
                if n:
                    store_act(n - 1, NK - 5 + n)
                for k in range(4):
                    sp.wait_ge(act_stored[k], 16 * (PASSES + (k < n)))
                with sp.Fori(a, min(b, PASSES - 1)) as q:
                    for k in range(4):
                        sp.wait_ge(s["v_split"], 4 * q + (k + 1))
                        sp.wait_ge(s["wf_ready"], 4 * q + (k + 1))
                        sp.sem_inc(s["slot_go"], 1)
                        load_v(k, 4 * q + (k + 4))
                        load_w(k, 4 * q + (k + 4))
            sp.dma_start(x1b, x1_d).then_inc(s["x1b_in"], 16)
            for tt in range(NT):
                sp.wait_ge(s["final_ready"], tt + 1)
                sp.dma_start(out_d[tt * P:(tt + 1) * P, :], x1b[:, tt, :]).then_inc(s["out_done"], 16)
            sp.wait_ge(s["out_done"], 16 * NT)

        @block.gpsimd
        def _(pool):
            link = chain(pool, s["pchain"])
            g = nc.gpsimd
            link(g.memset(ones[:], 1.0))
            link(g.memset(eps[:, 0:1], EPS))
            link(g.memset(eps[:, 1:2], HD * EPS))
            link(g.iota(iota128[:], [[1, P]], base=0, channel_multiplier=0, allow_small_or_imprecise_dtypes=True))
            link(g.iota(iota16[:], [[1, TOPK]], base=0, channel_multiplier=0, allow_small_or_imprecise_dtypes=True))
            link(g.affine_select(out=upto[:], in_=ones[:], compare_op=ALU.is_ge, fill=0.0, base=0,
                                 pattern=[[1, P]], channel_multiplier=-1))
            link(g.affine_select(out=after[:], in_=ones[:], compare_op=ALU.is_gt, fill=0.0, base=0,
                                 pattern=[[-1, P]], channel_multiplier=1))
            link(g.affine_select(out=from_on[:], in_=ones[:], compare_op=ALU.is_ge, fill=0.0, base=0,
                                 pattern=[[-1, P]], channel_multiplier=1))
            link(g.affine_select(out=ident[:], in_=ones[:], compare_op=ALU.is_equal, fill=0.0, base=0,
                                 pattern=[[-1, P]], channel_multiplier=1))
            link(g.memset(halves[:], 0.0))
            link(g.memset(halves[0:64, 0:64], 1.0))
            link(g.memset(halves[64:128, 64:128], 1.0))
            g.memset(cin[:, :, 0:CONV - 1], 0.0).then_inc(s["consts"], 1)
            zero = iota16[:, 0:1].broadcast_to([P, DC * P])
            for i, n in enumerate(SPLIT):
                pool.wait_ge(w_in[n % RING], 16 * (n // RING + 1))
                if i >= 2:
                    full(pool, LAST_USE[SPLIT[i - 2]])
                w = wring[:, n % RING].rearrange("p c n -> p (c n)")
                hi, lo = bhi[:, i % 2].rearrange("p c n -> p (c n)"), blo[:, i % 2].rearrange("p c n -> p (c n)")
                g.tensor_tensor(hi, w, zero, ALU.add).then_inc(s["bhi_ready"], 1)
                pool.wait_ge(s["bhi_ready"], i + 1)
                g.tensor_tensor(lo, w, hi.bitcast(F32), ALU.subtract).then_inc(s["blo_ready"], 1)
            full(pool, LAST_USE[SPLIT[-1]])
            pool.wait_ge(s["adt_ready"], 1)
            for t in range(NT):
                if t >= 2:
                    full(pool, f"segB{t - 2}")
                g.tensor_tensor(sega[:, t % 2], after[:].unsqueeze(1).broadcast_to([P, SSD_H, P]),
                                dts[:, 4, t, :].unsqueeze(2).broadcast_to([P, SSD_H, P]),
                                ALU.mult).then_inc(s["sega_ready"], 1)
                if t:
                    if t == 3:
                        full(pool, "ea1")
                    g.tensor_copy(adtb[:, t % 2], dts[:, 4, t, :].unsqueeze(2).broadcast_to(
                        [P, SSD_H, HD])).then_inc(s["adtb_ready"], 1)
            diag = SB_AT
            for h in range(SB_H + 1):
                if h < SB_H:
                    pool.wait_ge(s["nk_ready"], h + 1)
                    for a in diag:
                        v_ = nk[:, h % 2, a:a + P]
                        g.affine_select(out=v_, in_=v_, compare_op=ALU.is_gt, fill=0.0, base=0,
                                        pattern=[[1, P]], channel_multiplier=-1).then_inc(s["nkm_ready"], 1)
                if h:
                    pool.wait_ge(s["sb_w"], h)
                    for a in diag:
                        v_ = wt[:, (h - 1) % 2, a:a + P]
                        g.affine_select(out=v_, in_=v_, compare_op=ALU.is_gt, fill=0.0, base=0,
                                        pattern=[[1, P]], channel_multiplier=-1).then_inc(s["sb_wm"], 1)
            pool.wait_ge(s["hhi_ready"], 1)
            g.tensor_tensor(hlo[:], h2T[:, :, TG:T], hhi[:].bitcast(F32), ALU.subtract).then_inc(s["hlo_ready"], 1)
            wq = wring[:].rearrange("p a b c -> p (a b c)").rearrange("p (c n) -> p c n", c=DC)
            for h in range(PH):
                pool.wait_ge(s["wqhi_ready"], h + 1)
                g.tensor_tensor(wqlo[:, h % 2], wq[:, :, h * P:(h + 1) * P], wqhi[:, h % 2].bitcast(F32),
                                ALU.subtract).then_inc(s["wqlo_ready"], 1)

            def lower_u(k, i):
                pool.wait_ge(s["uhi_ready"], i + 1)
                g.tensor_tensor(ulo[:, k % 2], uraw[:, k], uhi[:, k % 2].bitcast(F32), ALU.subtract).then_inc(s["u_split"], 1)

            def gather(table, k, j, turn, used, first):
                if not first:
                    pool.wait_ge(row_in[k], 16 * turn)
                g.tensor_copy(idx4[:, k:k + 1], eidx[:, bass.ds(j, 1)]).then_inc(s["idx_ready"], 1)
                pool.wait_ge(s["idx_ready"], j + 1 + (0 if table is u_d else HK))
                if used is not None:
                    pool.wait_ge(s[used], j + (-3 if table is u_d else 1))
                    pool.sem_inc(s["row_go"], 1)
                g.indirect_dma_start(urow[k], None, table, bass.IndirectOffsetOnAxis(idx4[:, k:k + 1], 0)).then_inc(row_in[k], 16)

            def gather_u(k, j, turn):
                first = isinstance(j, int) and j < 4
                gather(u_d, k, j, turn, None if first else "dot_ready", first)

            def pass_u(q, a, j0):
                for k in range(4):
                    lower_u(k, 4 * q + k)
                    if j0 is not None:
                        gather_u((j0 + k) % 4, 4 * q + (j0 - 4 * a + k), q + ((j0 + k) // 4 - a))

            def weigh(q, a, tt, n):
                pool.wait_ge(s["hotC_ready"], 8 * q + (16 * tt - 8 * a + n + 1))
                g.tensor_tensor(hotB[:, 0], hotB[:, 0],
                                rT[:, 2, bass.ds(64 * q + (8 * n - 64 * a), 8)].unsqueeze(2).broadcast_to([P, 8, P]),
                                ALU.mult).then_inc(s["hotB_even"], 1)
            for t in range(NT):
                a, b = R[t]
                if t == 1:
                    pool.wait_ge(s["eidx_ready"], 1)
                    pass_u(a, a, 0)
                    with pool.Fori(a + 1, b) as q:
                        pass_u(q, a, 0)
                else:
                    with pool.Fori(a, b) as q:
                        pass_u(q, a, R_GATHER[t])
                if t:
                    a, b = H[t - 1]
                    j0 = H_GATHER[t - 1]

                    def pass_h(q):
                        for k in range(4):
                            weigh(q, a, t - 1, 2 * k)
                            for n in (2 * k, 2 * k + 1):
                                gather_u((j0 + n) % 4, 8 * q + (j0 - 8 * a + n), 2 * q + ((j0 + n) // 4 - 2 * a))
                            lower_u(k, 4 * q + k)
                    pool.wait_ge(s["rT_ready"], t)
                    with pool.Fori(a, b) as q:
                        pass_h(q)
            with pool.Fori(H[-1][1], PASSES - 1) as q:
                pass_u(q, 0, None)

            def weights(k, q):
                i = 4 * q + k
                gather(v_d.rearrange("i e d -> (i e) d"), k, i, HK // 4 + q, "vrow_free", False)
                pool.wait_ge(a_in[k], 16 * q + 16)
                pool.wait_ge(g_in[k], 16 * q + 16)
                pool.wait_ge(s["w_ready"], i + 1)
                g.tensor_tensor(wf[:, k, :], aring[:, k, :], gring[:, k, :], ALU.mult).then_inc(s["wf_ready"], 1)
            pool.wait_ge(s["dot_ready"], HK)
            for n, (a, b) in enumerate(zip(LAST_U, LAST_U[1:])):
                if n < 4:
                    lower_u(n, NK - 4 + n)
                with pool.Fori(a, b) as q:
                    for k in range(4):
                        weights(k, q)

        @block.tensor
        def _(pe):
            def mm(out, lhsT, rhs, start=True, stop=True):
                return nc.tensor.matmul(out, lhsT, rhs, start=start, stop=stop)

            def job(name):
                n = JOB[name]
                if n >= 8:
                    pe.wait_ge(job_free[n % 8], n // 8)
                return bank(name)

            other_rows = chain(pe, s["rows_done"])

            def done(ins, name):
                ins.then_inc(job_full[JOB[name] % 8], 1)

            def chunk(n):
                pe.wait_ge(w_in[n % RING], 16 * (n // RING + 1))
                return wring[:, n % RING, :, :]

            def squares(name, ready, width):
                o = job(name)
                for c in range(DC):
                    pe.wait_ge(s[ready], c + 1)
                    last = mm(o[:, 0:width], ones[:], sq[:, c % 2, 0:width], c == 0, c == DC - 1)
                    if c < DC - 1:
                        last.then_inc(s["sq_used"], 1)
                    else:
                        done(last, name)

            def to_rows(name, all_name, scales, tiles):
                o = job(name)
                freed(pe, all_name)
                for t in range(tiles):
                    last = mm(o[:, t:t + 1], scales[0:1, t * P:(t + 1) * P], ones[0:1, 0:1])
                done(last, name)

            def channels(name, n, rhs, width):
                if n in SPLIT:
                    o, i = job(name), SPLIT.index(n)
                    pe.wait_ge(s["xlo_ready"], DC)
                    pe.wait_ge(s["bhi_ready"], i + 1)
                    for c in range(DC):
                        mm(o, bhi[:, i % 2, c, :], xhi[:, c, :], c == 0, False)
                        mm(o, bhi[:, i % 2, c, :], xlo[:, c, :], False, False)
                    pe.wait_ge(s["blo_ready"], i + 1)
                    for c in range(DC):
                        last = mm(o, blo[:, i % 2, c, :], xhi[:, c, :], False, c == DC - 1)
                    done(last, name)
                    return
                o, w = job(name), chunk(n)
                for c in range(DC):
                    if n == 0:
                        pe.wait_ge(s["xg_ready"], c + 1)
                    last = mm(o[:, 0:width], w[:, c, :], rhs[:, c, :], c == 0, c == DC - 1)
                done(last, name)

            def tokens(name, t, n, count, lhs):
                o = job(name)
                for i in range(count):
                    chunk(n + i)
                a = n % RING
                for c in range(DC):
                    last = mm(o[:, 0:count * P], lhs[:, c, t * P:(t + 1) * P], wring[:, a:a + count, c, :],
                              c == 0, c == DC - 1)
                done(last, name)

            pe.wait_ge(s["consts"], 1)
            for i in range(CC):
                channels(f"xbc{i}", CHUNK_OF["xbc"] + i, xg, T)
                if i == 1:
                    squares("ssqx", "sqx_ready", T)
                if i == 2:
                    to_rows("rowx", "ssqx", rsB, NT)
            o = job("dt")
            pe.wait_ge(s["wdt_in"], 48)
            for t in range(NT):
                for c in range(DC):
                    last = mm(o[:, SSD_H * t:SSD_H * (t + 1)], xg[:, c, t * P:(t + 1) * P], wdt[:, c, :],
                              c == 0, c == DC - 1)
            done(last, "dt")
            for kind in ("q", "k"):
                for i in range(3):
                    channels(f"{kind}{i}", CHUNK_OF[kind] + i, xg, T)
            for t in range(NT):
                tokens(f"v{t}", t, CHUNK_OF["v"], 3, xg)
            for kind, count in (("z", 3), ("qm", 2)):
                for i in range(count):
                    channels(f"{kind}{i}", CHUNK_OF[kind] + i, xg, T)
            squares("ssqm", "sqm_ready", M)
            pe.wait_ge(s["memg_ready"], DC)
            for i in range(2):
                channels(f"mk{i}", CHUNK_OF["mk"] + i, memT, M)
            to_rows("rowm", "ssqm", rmB, MT)
            for t in range(MT):
                tokens(f"mv{t}", t, CHUNK_OF["mv"], 2, memT)
            for i in range(2):
                o = job(f"mkss{i}")
                pe.wait_ge(s["mksq_ready"], i + 1)
                done(mm(o[:, 0:M], halves[:], mksq[:, i, :]), f"mkss{i}")
            o = job("qmss")
            pe.wait_ge(s["qsq_ready"], 2)
            for t in range(NT):
                for i in range(2):
                    last = mm(o[:, 4 * t + 2 * i:4 * t + 2 * i + 2], qsq[:, i, t * P:(t + 1) * P], halves[:, 0:P:HD])
            done(last, "qmss")

            def ssd(t):
                cols = slice(t * P, (t + 1) * P)
                o = job(f"tr{t}")
                for i in range(4):
                    last = nc.tensor.transpose(o[:, i * P:(i + 1) * P], xcT[:, i, cols], ident[:])
                done(last, f"tr{t}")
                o = job(f"cb{t}")
                for g in range(SSD_G):
                    rows_ = slice(HD * g, HD * (g + 1))
                    last = mm(o[:, g * P:(g + 1) * P], xcT[rows_, 3, cols], xcT[rows_, 4, cols])
                    if g == 0:
                        other_rows(last)
                done(last, f"cb{t}")
                o = job(f"dec{t}")
                if t == 0:
                    pe.wait_ge(s["adt_ready"], 1)
                mm(o[:, 0:SSD_H], after[:], dts[:, 4, t, :])
                done(mm(o[:, SSD_H:2 * SSD_H], ones[:], dts[:, 4, t, :]), f"dec{t}")
                pe.wait_ge(s["sega_ready"], t + 1)
                for half, name in enumerate((f"segA{t}", f"segB{t}")):
                    o = job(name)
                    for i in range(3):
                        last = mm(o[:, i * P:(i + 1) * P], sega[:, t % 2, 3 * half + i, :], upto[:])
                    done(last, name)
                if t:
                    o = job(f"ea{t}")
                    pe.wait_ge(s["adtb_ready"], t)
                    for g in range(SSD_G):
                        for i in range(HPG):
                            last = mm(o[HD * g:HD * (g + 1), i * P:(i + 1) * P], adtb[:, t % 2, HPG * g + i, :], upto[:])
                    done(last, f"ea{t}")
                if t < NT - 1:
                    o = job(f"st{t}")
                    pe.wait_ge(s["xdd_ready"], t + 1)
                    for g in range(SSD_G):
                        last = mm(o[HD * g:HD * (g + 1), 0:HPG * HD], xn[:, t, SSD_W + HD * g:SSD_W + HD * (g + 1)],
                                  xdd[:, HPG * g:HPG * (g + 1), :])
                    done(last, f"st{t}")

            def memory(c, t):
                if t < NT:
                    o = job(f"sc{c}{t}")
                    for e in range(2):
                        r_ = slice(HD * e, HD * (e + 1))
                        last = mm(o[:, e * M:(e + 1) * M], qmT[r_, c, t * P:(t + 1) * P], mkT[r_, c, :])
                        if e == 0:
                            other_rows(last)
                    done(last, f"sc{c}{t}")
                for u in turned_at(t):
                    n = NT * c + u
                    o = job(f"pT{c}{u}")
                    pe.wait_ge(s["pn_ready"], n + 1)
                    for e in range(2):
                        for m in range(MT):
                            last = nc.tensor.transpose(o[:, (2 * e + m) * P:(2 * e + m + 1) * P],
                                                       pr[:, n % 3, e, m * P:(m + 1) * P], ident[:])
                    done(last, f"pT{c}{u}")
                if t == NT:
                    o = job(f"ym{c}")
                    freed(pe, f"pT{c}{NT - 1}")
                    for e in range(2):
                        for m in range(MT):
                            last = mm(o[HD * e:HD * (e + 1), :], mvrow[:, m, HD * (2 * c + e):HD * (2 * c + e + 1)],
                                      pT[:, e, m, :], m == 0, m == MT - 1)
                    done(last, f"ym{c}")
            pe.wait_ge(s["xc_ready"], CC)
            pe.wait_ge(s["mkn_ready"], 2)
            freed(pe, f"mv{MT - 1}")
            for kind, c, t in STEPS:
                if kind == "ssd":
                    ssd(t)
                else:
                    memory(c, t)
            pe.wait_ge(s["m_ready"], NT)
            pe.wait_ge(s["cdec_ready"], NT - 1)
            freed(pe, f"st{NT - 2}")
            for i in range(SC):
                o = job(f"y{i}")
                for e in range(2):
                    h = 2 * i + e
                    g, hh = h // HPG, h % HPG
                    for t in range(NT):
                        out = o[HD * e:HD * (e + 1), t * P:(t + 1) * P]
                        last = mm(out, xn[:, t, HD * h:HD * (h + 1)], lm[:, t, h, :], True, t == 0)
                        if t:
                            last = mm(out, state[HD * g:HD * (g + 1), t, hh, :],
                                      cdec[HD * g:HD * (g + 1), t, hh, :], False, True)
                    if h == HPG - 1:
                        other_rows(last)
                done(last, f"y{i}")
            o = job("ssqy")
            for i in range(SC):
                pe.wait_ge(s["sqy_ready"], i + 1)
                last = mm(o, ones[:], cin[:, i, 0:T], i == 0, i == SC - 1)
            done(last, "ssqy")

            o = job("ssqym")
            for i in range(2):
                pe.wait_ge(s["sqym_ready"], i + 1)
                last = mm(o, ones[:], sq[:, i, :], i == 0, i == 1)
            done(last, "ssqym")

            for b in range(8):
                pe.wait_ge(job_free[b], len([n for n in range(len(JOBS)) if n % 8 == b]))
            zb = psum[:, 0:3, :].rearrange("p b n -> p (b n)")
            sbk = psum[:, 3:6, :].rearrange("p b n -> p (b n)")

            def scores(h):
                if h:
                    pe.wait_ge(s["z_read"], h)
                e, c = h % 2, h // 2
                for j in range(NT):
                    last = mm(zb[:, SB_AT[j]:SB_AT[j] + T - j * P], kT[HD * e:HD * (e + 1), c, j * P:(j + 1) * P],
                              qT[HD * e:HD * (e + 1), c, j * P:T])
                last.then_inc(s["z_full"], 1)

            def kept(h):
                pe.wait_ge(s["nkm_ready"], 4 * (h + 1))
                if h:
                    pe.wait_ge(s["arg_ready"], h)
                for j in range(NT):
                    for i in range(j, NT):
                        last = mm(sbk[:, SB_AT[j] + (i - j) * P:SB_AT[j] + T - j * P],
                                  (from_on if i == j else ones)[:], nk[:, h % 2, SB_AT[i]:SB_AT[i] + T - i * P],
                                  i == j, i == NT - 1)
                last.then_inc(s["kept_full"], 1)

            def values(h):
                pe.wait_ge(s["sb_wm"], 4 * (h + 1))
                e, c = h % 2, h // 2
                if c == 2 and e == 0:
                    pe.wait_ge(s["ysb_ready"], 1)
                for j in range(NT):
                    last = mm(psum[HD * e:HD * (e + 1), 6 + c % 2, j * P:T], vrow[:, j, HD * h:HD * (h + 1)],
                              wt[:, h % 2, SB_AT[j]:SB_AT[j] + T - j * P], j == 0, j == NT - 1)
                last.then_inc(s["av_full"], 1)
            scores(0)
            for h in range(SB_H):
                if h < SB_H - 1:
                    scores(h + 1)
                kept(h)
                if h:
                    values(h - 1)

            def project(n, channels_):
                t, half = divmod(n, 2)
                for c in channels_:
                    last = mm(psum[:, 1 + n % 4, :], ymix[:, c, t * P:(t + 1) * P],
                              wout[:, c, half * 512:(half + 1) * 512], c == 0, c == 5)
                return last
            early, late = (0, 1, 2, 6, 7), (3, 4, 5)
            pe.wait_ge(s["wout_in"], 16)
            pe.wait_ge(s["z_read"], SB_H)
            pe.wait_ge(s["arg_ready"], SB_H)
            project(0, early)
            values(SB_H - 1)
            for n in range(1, 4):
                project(n, early)
            for i in range(SC):
                pe.wait_ge(s["sqs_ready"], i + 1)
                last = mm(psum[:, 0, :], ones[:], sqs[:, i, :], i == 0, i == SC - 1)
            last.then_inc(s["sbss_full"], 1)
            pe.wait_ge(s["ymix_ready"], 8)
            wq = wring[:].rearrange("p a b c -> p (a b c)").rearrange("p (c n) -> p c n", c=DC)
            for t in range(NT + 1):
                if t < NT:
                    for n in (2 * t, 2 * t + 1):
                        if n >= 4:
                            pe.wait_ge(s["x1_ready"], n - 3)
                        project(n, early + late if n >= 4 else late).then_inc(s["o_full"], 1)
                if t == NT:
                    pe.wait_ge(s["wq_in"], 16)
                    pe.wait_ge(s["h2T_ready"], 2)
                    for h in range(PH):
                        for c in range(DC):
                            last = mm(psum[:, 7 * (h // 4), (h % 4) * P:(h % 4 + 1) * P], wq[:, c, h * P:(h + 1) * P],
                                      h2T[:, c, 0:P], c == 0, c == DC - 1)
                        if h % 4 == 3:
                            last.then_inc(s["pq_full"], 1)
                if t:
                    pe.wait_ge(s["h2row_ready"], t)
                    for half in range(2):
                        n = 2 * (t - 1) + half
                        if n >= 2:
                            pe.wait_ge(s["h2T_ready"], n - 1)
                        for i in range(4):
                            c = 4 * half + i
                            last = nc.tensor.transpose(psum[:, 5 + half, i * P:(i + 1) * P],
                                                       h2row[:, min(t - 1, 1), c * P:(c + 1) * P], ident[:])
                        last.then_inc(s["h2t_full"], 1)

            pe.wait_ge(s["x1_ready"], 2 * NT)
            pe.wait_ge(s["h2T_ready"], 2 * NT)
            pe.wait_ge(s["keys_in"], 16)
            pe.wait_ge(s["pq_ready"], 2)

            def key_scores(t):
                if t:
                    pe.wait_ge(s["sco_ready"], 4 * t)
                if t > 2:
                    pe.wait_ge(s["g_free"], 16 * (t - 2) + 2)
                for c in range(2):
                    r_ = slice(HD * c, HD * (c + 1))
                    for i in range(PH // 2):
                        for h in (2 * i, 2 * i + 1):
                            a = (2 * (h % 2) + c) * P
                            last = mm(psum[:, 4 + i, a:a + P], pqT[r_, h, t * P:(t + 1) * P], keysT[r_, h, :])
                        if c:
                            last.then_inc(s["sco_full"], 1)
                    if c == 0:
                        other_rows(last)

            def turned(tt):
                pe.wait_ge(s["routed_ready"], tt + 2)
                if tt:
                    pe.wait_ge(s["rT_ready"], tt)
                for i in range(3):
                    last = nc.tensor.transpose(psum[:, 2, i * P:(i + 1) * P], routed[:, i, :], ident[:])
                last.then_inc(s["rT_full"], 1)

            def up(k, i):
                pe.wait_ge(s["uhi_ready"], i + 1)
                pe.wait_ge(s["act_ready"], i + 1)
                out = psum[:, k % 2, 0:TD]
                for c in range(DC):
                    mm(out, uhi[:, k % 2, c, :], hhi[:, c, :], c == 0, False)
                    mm(out, uhi[:, k % 2, c, :], hlo[:, c, :], False, False)
                pe.wait_ge(s["u_split"], i + 1)
                for c in range(DC):
                    last = mm(out, ulo[:, k % 2, c, :], hhi[:, c, :], False, c == DC - 1)
                last.then_inc(s["p1_done"], 1)

            def ups(a, b):
                if a == b:
                    return
                with pe.Fori(a, b) as q:
                    for k in range(4):
                        up(k, 4 * q + k)

            def gates(q, a, tt, n):
                k = n % 2
                pe.wait_ge(s["hotA_ready"], 8 * q + (16 * tt - 8 * a + n + 1))
                pe.wait_ge(s["hotB_odd" if k else "hotB_even"], 4 * q + (8 * tt - 4 * a + n // 2 + 1))
                pe.wait_ge(s["g_free"], 8 * q + (16 * tt - 8 * a + n + 1))
                for i in range(8):
                    last = mm(psum[:, 4 + 2 * k + i // 4, (i % 4) * P:(i % 4 + 1) * P], hotB[:, k, i, :], hotA[:, k, i, :])
                last.then_inc(s["g_full"], 1)
            pe.sem_inc(s["g_full"], 2)
            pe.sem_inc(s["p1_done"], 2)
            key_scores(0)
            pe.wait_ge(s["hlo_ready"], 1)
            for h in range(PH):
                pe.wait_ge(s["wqhi_ready"], h + 1)
                if h < 4:
                    pe.wait_ge(s["sco_ready"], h + 1)
                if h >= 4:
                    pe.wait_ge(s["pq_ready"], 2 + h - 3)
                out = psum[:, 4 + h % 4, 0:TD]
                for c in range(DC):
                    mm(out, wqhi[:, h % 2, c, :], hhi[:, c, :], c == 0, False)
                    mm(out, wqhi[:, h % 2, c, :], hlo[:, c, :], False, False)
                pe.wait_ge(s["wqlo_ready"], h + 1)
                for c in range(DC):
                    last = mm(out, wqlo[:, h % 2, c, :], hhi[:, c, :], False, c == DC - 1)
                last.then_inc(s["pq_full"], 1)
            pe.wait_ge(s["pq_ready"], PH + 2)
            for t in range(NT):
                a, b = R[t]
                if t < NT - 1:
                    ups(a, R_SCORES[t])
                    key_scores(t + 1)
                    a = R_SCORES[t]
                if t:
                    ups(a, b - 1)
                    turned(t - 1)
                    a = b - 1
                ups(a, b)
                if t:
                    a, b = H[t - 1]
                    pe.wait_ge(s["sco_ready"], 4 * min(t + 2, NT))
                    with pe.Fori(a, b) as q:
                        for k in range(4):
                            gates(q, a, t - 1, 2 * k)
                            gates(q, a, t - 1, 2 * k + 1)
                            up(k, 4 * q + k)
            pe.wait_ge(s["g_free"], 16 * DT + 2)
            pe.wait_ge(s["zero_ready"], 1)
            for b in range(2, 8):
                mm(psum[:, b, :], zr[:, 0:P], zr[:])
            pe.sem_inc(s["p2_done"], 4)
            ups(H[-1][1], PASSES - 1)

            def down(k, i):
                pe.wait_ge(s["v_split"], i + 1)
                pe.wait_ge(s["w_ready"], i + 5)
                for t in range(DT):
                    for l_, r_ in ((whi, vhi), (whi, vlo), (wlo, vhi)):
                        for half in range(2):
                            last = nc.tensor.matmul(psum[:, 2 + 2 * t + half, :], l_[:, k, t * P:(t + 1) * P],
                                                    r_[:, k, half * 512:(half + 1) * 512], start=False, stop=True,
                                                    skip_group_check=True)
                last.then_inc(s["p2_done"], 1)
            for n, (a, b) in enumerate(zip(LAST_U, LAST_U[1:])):
                if n < 4:
                    up(n, NK - 4 + n)
                with pe.Fori(a, b) as q:
                    for k in range(4):
                        down(k, 4 * q + k)

        @block.scalar
        def _(act):
            a_ = nc.scalar.activation
            link = chain(act, s["achain"])

            def exp_ln_tables():
                act.preload_act_table_set("natural_log_exp_and_others")
            exp_ln_tables()
            for c in range(DC):
                act.wait_ge(s["xg_ready"], c + 1)
                a_(xhi[:, c, :], xg[:, c, :], ACT.Copy).then_inc(s["xhi_ready"], 1)
            for c in range(DC):
                act.wait_ge(s["xT_in0" if c < 2 else "xT_in1"], 16)
                if c >= 2:
                    act.wait_ge(s["sq_used"], c - 1)
                a_(sq[:, c % 2, :], xT[:, c, :], ACT.Square).then_inc(s["sqx_ready"], 1)
            act.wait_ge(s["consts"], 1)
            full(act, "ssqx")
            link(a_(rsB[:], bank("ssqx"), ACT.Ln, scale=1.0 / D, bias=eps[:, 0:1]))
            free(a_(rsB[:], rsB[:], ACT.Exp, scale=-0.5), "ssqx")
            full(act, "rowx")
            free(a_(rowr[:, 0:NT], bank("rowx")[:, 0:NT], ACT.Copy), "rowx")
            act.wait_ge(s["wdt_in"], 48)
            a_(alog[:], alog[:], ACT.Exp).then_inc(s["dtp"], 1)
            act.wait_ge(s["udt"], 1)
            link(a_(dts[:, 2], dts[:, 1], ACT.Exp, scale=-1.0))
            a_(dts[:, 2], dts[:, 2], ACT.Ln, bias=1.0).then_inc(s["dtp"], 1)
            for i in range(CC):
                act.wait_ge(s["conv_ready"], i + 1)
                a_(xcT[:, i, :], xcT[:, i, :], ACT.Silu).then_inc(s["xc_ready"], 1)
            for t in range(NT):
                full(act, f"v{t}")
                free(a_(vrow[:, t, :], bank(f"v{t}")[:, 0:SB_W], ACT.Copy, scale=rowr[:, t:t + 1]), f"v{t}")
            for i in range(SC):
                freed(act, f"z{i}")
                a_(zT[:, i, :], zT[:, i, :], ACT.Silu).then_inc(s["silu_ready"], 1)
            exp_ln_tables()
            act.wait_ge(s["memT_in"], 16)
            full(act, "ssqx")
            for c in range(DC):
                if c >= 2:
                    act.wait_ge(s["sq_used"], DC - 1 + c - 1)
                a_(sq[:, c % 2, 0:M], memT[:, c, :], ACT.Square).then_inc(s["sqm_ready"], 1)
            full(act, "ssqm")
            link(a_(rmB[:], bank("ssqm")[:, 0:M], ACT.Ln, scale=1.0 / D, bias=eps[:, 0:1]))
            free(a_(rmB[:], rmB[:], ACT.Exp, scale=-0.5), "ssqm")
            for i in range(2):
                freed(act, f"qm{i}")
                a_(qsq[:, i, :], qmT[:, i, :], ACT.Square).then_inc(s["qsq_ready"], 1)
            for i in range(2):
                freed(act, f"mk{i}")
                a_(mksq[:, i, :], mkT[:, i, :], ACT.Square).then_inc(s["mksq_ready"], 1)
            full(act, "rowm")
            free(a_(rowr[:, 4:4 + MT], bank("rowm")[:, 0:MT], ACT.Copy), "rowm")
            for t in range(MT):
                full(act, f"mv{t}")
                if t == 0:
                    freed(act, "rowm")
                free(a_(mvrow[:, t, :], bank(f"mv{t}")[:, 0:MEM_W], ACT.Copy, scale=rowr[:, 4 + t:5 + t]), f"mv{t}")
            for i in range(2):
                full(act, f"mkss{i}")
                link(a_(mksq[:, i, :], bank(f"mkss{i}")[:, 0:M], ACT.Ln, scale=1.0 / HD, bias=eps[:, 0:1]))
                free(a_(mksq[:, i, :], mksq[:, i, :], ACT.Exp, scale=-0.5), f"mkss{i}")
            full(act, "qmss")
            link(a_(rq[:], bank("qmss")[:, 0:16], ACT.Ln, bias=eps[:, 1:2]))
            free(a_(rq[:], rq[:], ACT.Exp, scale=-0.5), "qmss")

            def ssd(t):
                full(act, f"tr{t}")
                free(a_(xn[:, t, :], bank(f"tr{t}"), ACT.Copy), f"tr{t}")
                full(act, f"dec{t}")
                free(a_(dec[:, t, :], bank(f"dec{t}")[:, 0:12], ACT.Exp), f"dec{t}")
                for half, name in enumerate((f"segA{t}", f"segB{t}")):
                    full(act, name)
                    free(a_(lm[:, t, 3 * half:3 * half + 3, :], bank(name)[:, 0:3 * P].rearrange("p (h l) -> p h l", h=3),
                            ACT.Exp), name)
                if t:
                    full(act, f"ea{t}")
                    free(a_(cdec[:, t], bank(f"ea{t}")[:, 0:3 * P].rearrange("p (h l) -> p h l", h=3), ACT.Exp), f"ea{t}")

            def turned(n):
                c, t = divmod(n, NT)
                full(act, f"pT{c}{t}")
                if n == NT:
                    full(act, "ym0")
                free(a_(pT[:, :, :, t * P:(t + 1) * P], bank(f"pT{c}{t}").rearrange("p (e m l) -> p e m l", e=2, m=2),
                        ACT.Copy), f"pT{c}{t}")

            def memory(c, t):
                n = NT * c + t
                if t < NT:
                    act.wait_ge(s["smax_ready"], n + 1)
                    if n >= 3:
                        c2, t2 = divmod(n - 3, NT)
                        full(act, f"pT{c2}{t2}")
                    o = bank(f"sc{c}{t}")
                    for e in range(2):
                        ins = a_(pr[:, n % 3, e, :], o[:, e * M:(e + 1) * M], ACT.Exp,
                                 scale=rq[:, 4 * t + 2 * c + e:4 * t + 2 * c + e + 1], bias=mstat[:, 1, n, e:e + 1],
                                 accum_out=mstat[:, 2, n, e:e + 1])
                        if e == 0:
                            link(ins)
                    free(ins, f"sc{c}{t}")
                for u in turned_at(t):
                    turned(NT * c + u)
                if t == NT:
                    freed(act, f"ym{c}")
                    if c == 0:
                        full(act, "ssqm")
                    a_(sq[:, c, :], ymix[:, 6 + c, :], ACT.Square).then_inc(s["sqym_ready"], 1)
            for kind, c, t in STEPS:
                if kind == "ssd":
                    ssd(t)
                else:
                    memory(c, t)
            for i in range(SC):
                act.wait_ge(s["yg_ready"], i + 1)
                a_(cin[:, i, 0:T], yg[:, i, :], ACT.Square).then_inc(s["sqy_ready"], 1)
            full(act, "ssqy")
            link(a_(rsB[:], bank("ssqy"), ACT.Ln, scale=1.0 / SSD_W, bias=eps[:, 0:1]))
            free(a_(rsB[:], rsB[:], ACT.Exp, scale=-0.5), "ssqy")

            full(act, "ssqym")
            rB2 = xcT[:, 4, :]
            link(a_(rB2, bank("ssqym"), ACT.Ln, scale=1.0 / MEM_W, bias=eps[:, 0:1]))
            free(a_(rB2, rB2, ACT.Exp, scale=-0.5), "ssqym")

            act.wait_ge(s["ymix_ready"], 5)
            zb = psum[:, 0:3, :].rearrange("p b n -> p (b n)")[:, 0:SB_N]

            def front(h):
                k = h % 2
                act.wait_ge(s["z_full"], h + 1)
                if h >= 2:
                    act.wait_ge(s["arg_ready"], h - 1)
                a_(zs[:, k, :], zb, ACT.Copy, scale=HD ** -0.5).then_inc(s["zs_ready"], 1)
                ins = a_(lk[:, k, :], zb, ACT.Abs, scale=HD ** -0.5)
                ins.then_inc(s["z_read"], 1)
                act.wait_ge(s["z_read"], h + 1)
                link(a_(lk[:, k, :], lk[:, k, :], ACT.Exp, scale=-1.0))
                a_(lk[:, k, :], lk[:, k, :], ACT.Ln, bias=1.0).then_inc(s["lk_ready"], 1)
            front(0)
            for h in range(SB_H):
                if h < SB_H - 1:
                    front(h + 1)
                act.wait_ge(s["arg_ready"], h + 1)
                a_(wt[:, h % 2, :], wt[:, h % 2, :], ACT.Exp).then_inc(s["sb_w"], 1)
            for i in range(SC):
                act.wait_ge(s["ysb_ready"], i + 1)
                a_(sqs[:, i, :], ysb[:, i, :], ACT.Square).then_inc(s["sqs_ready"], 1)
            act.wait_ge(s["sbss_full"], 1)
            link(a_(rbB[:], psum[:, 0, :], ACT.Ln, scale=1.0 / SB_W, bias=eps[:, 0:1]))
            a_(rbB[:], rbB[:], ACT.Exp, scale=-0.5).then_inc(s["rbB_ready"], 1)

            def turned_rows(n):
                t, half = divmod(n, 2)
                act.wait_ge(s["h2t_full"], n + 1)
                a_(h2T[:, 4 * half:4 * half + 4, t * P:(t + 1) * P],
                   psum[:, 5 + half, :].rearrange("p (c l) -> p c l", c=4), ACT.Copy).then_inc(s["h2T_ready"], 1)
            for t in range(NT):
                act.wait_ge(s["x1_ready"], 2 * t + 2)
                if t >= 2:
                    act.wait_ge(s["h2t_full"], 2 * t)
                link(a_(h2row[:, min(t, 1), :], x1[:, t, :], ACT.Square, accum_out=rowr2[:, t:t + 1]))
                link(a_(rowr2[:, t:t + 1], rowr2[:, t:t + 1], ACT.Ln, scale=1.0 / D, bias=eps[:, 0:1]))
                a_(rowr2[:, t:t + 1], rowr2[:, t:t + 1], ACT.Exp, scale=-0.5).then_inc(s["r2_ready"], 1)
                if t:
                    turned_rows(2 * t - 2)
                    turned_rows(2 * t - 1)
            for i in range(2):
                act.wait_ge(s["pq_full"], i + 1)
                a_(pqT[:, 4 * i:4 * i + 4, 0:P], psum[:, 7 * i, :].rearrange("p (h l) -> p h l", h=4), ACT.Copy).then_inc(s["pq_ready"], 1)
            turned_rows(2 * NT - 2)
            turned_rows(2 * NT - 1)

            act.wait_ge(s["h2row_ready"], NT)
            act.wait_ge(s["h2T_ready"], 2 * NT)
            act.wait_ge(s["x1_stored"], 16)
            a_(hhi[:], h2T[:, :, TG:T], ACT.Copy).then_inc(s["hhi_ready"], 1)
            act.wait_ge(s["wq_in"], 16)
            wq = wring[:].rearrange("p a b c -> p (a b c)").rearrange("p (c n) -> p c n", c=DC)

            def upper_wq(h):
                if h >= 2:
                    act.wait_ge(s["pq_full"], h + 1)
                a_(wqhi[:, h % 2], wq[:, :, h * P:(h + 1) * P], ACT.Copy).then_inc(s["wqhi_ready"], 1)
            upper_wq(0)
            upper_wq(1)
            act.sem_inc(s["g_free"], 2)
            act.sem_inc(s["act_ready"], 2)

            def key_scores(t, i):
                n = 4 * t + i
                act.wait_ge(s["sco_full"], n + 1)
                if t:
                    act.wait_ge(s["sco_used"], n - 3)
                a_(sco[:, 2 * i:2 * i + 2, :, :], psum[:, 4 + i, :].rearrange("p (h c n) -> p h c n", h=2, c=2),
                   ACT.Copy).then_inc(s["sco_ready"], 1)

            def softmax(t):
                act.wait_ge(s["soft_in"], t + 1)
                a_(sm[:, 1], sm[:, 0], ACT.Exp).then_inc(s["soft_out"], 1)
                act.preload_act_table(ACT.Gelu)

            def routed_turned(tt):
                act.wait_ge(s["rT_full"], tt + 1)
                if tt:
                    act.wait_ge(s["g_full"], 16 * tt + 2)
                a_(rT[:], psum[:, 2, 0:3 * P].rearrange("p (r l) -> p r l", r=3), ACT.Copy).then_inc(s["rT_ready"], 1)

            def upper_u(k, q):
                act.wait_ge(u_in[k], 16 * q + 16)
                act.wait_ge(s["p1_done"], 4 * q + (k + 1))
                a_(uhi[:, k % 2], uraw[:, k], ACT.Copy).then_inc(s["uhi_ready"], 1)

            def activations(k, q):
                before = (k - 1) % 4
                act.wait_ge(s["p1_done"], 4 * q + (k + 2))
                act.wait_ge(act_stored[before], 16 * q + (16 if k else 0))
                a_(act_s[:, before, :], psum[:, before % 2, 0:TD], ACT.Gelu).then_inc(s["act_ready"], 1)

            def tile(k, q):
                upper_u(k, q)
                if not (isinstance(q, int) and q == 0 and k == 0):
                    activations(k, q)

            def tiles(a, b):
                if a == b:
                    return
                with act.Fori(a, b) as q:
                    for k in range(4):
                        tile(k, q)

            def weigh(q, a, tt, n):
                act.wait_ge(s["hotC_ready"], 8 * q + (16 * tt - 8 * a + n + 1))
                for i in range(8):
                    ins = a_(hotB[:, 1, i, :], hotB[:, 1, i, :], ACT.Copy, scale=rT[:, 2, bass.ds(64 * q + (8 * n + i - 64 * a), 1)])
                ins.then_inc(s["hotB_odd"], 1)

            def stage_gates(q, a, tt, n):
                k = n % 2
                act.wait_ge(s["g_full"], 8 * q + (16 * tt - 8 * a + n + 3))
                for e in range(2):
                    ins = a_(stage[e].rearrange("j i t -> j t i")[:, bass.ds(64 * q + (8 * n - 64 * a), 8), :],
                             psum[:, 4 + 2 * k:6 + 2 * k, :].rearrange("p b (t i) -> p (b t) i", t=4)[
                                 :, :, 64 * e:64 * (e + 1)], ACT.Copy)
                ins.then_inc(s["g_free"], 1)
            for i in range(PH // 2):
                key_scores(0, i)
            act.preload_act_table(ACT.Gelu)
            for h in range(PH):
                act.wait_ge(s["pq_full"], h + 3)
                a_(pqT[:, h, P:T], psum[:, 4 + h % 4, 0:TD], ACT.Copy).then_inc(s["pq_ready"], 1)
                if h < PH - 2:
                    upper_wq(h + 2)
            for t in range(NT):
                a, b = R[t]
                if t < NT - 1:
                    if t:
                        tiles(a, R_SCORES[t])
                    a = R_SCORES[t] + 1
                    for k in range(4):
                        key_scores(t + 1, k)
                        tile(k, a - 1)
                tiles(a, R_SOFTMAX[t])
                softmax(t)
                if t == 0:
                    tiles(R_SOFTMAX[0], b)
                else:
                    tiles(R_SOFTMAX[t], b - 1)
                    routed_turned(t - 1)
                    tiles(b - 1, b)
                    if t >= 2:
                        act.wait_ge(s["gate_stored"], 16 * PIECES * (t - 1))
                    a, b = H[t - 1]
                    with act.Fori(a, b) as q:
                        for k in range(4):
                            upper_u(k, q)
                            weigh(q, a, t - 1, 2 * k + 1)
                            activations(k, q)
                            stage_gates(q, a, t - 1, 2 * k)
                            stage_gates(q, a, t - 1, 2 * k + 1)
            tiles(H[-1][1], PASSES - 1)
            act.wait_ge(s["dot_ready"], HK)
            a_(wrow[:], dots[:], ACT.Gelu).then_inc(s["ge_ready"], 1)

            def upper_v(k, q):
                act.wait_ge(v_in[k], 16 * q + 16)
                act.wait_ge(s["p2_done"], 4 * q + (k + 1))
                a_(vhi[:, k, :], vraw[:, k, :], ACT.Copy).then_inc(s["vhi_ready"], 1)

            def upper_w(k, q):
                act.wait_ge(s["wf_ready"], 4 * q + (k + 1))
                a_(whi[:, k, :], wf[:, k, :], ACT.Copy).then_inc(s["whi_ready"], 1)
            for n, (a, b) in enumerate(zip(LAST_U, LAST_U[1:])):
                if n < 4:
                    tile(n, PASSES - 1)
                else:
                    activations(0, PASSES)
                with act.Fori(a, b) as q:
                    for k in range(4):
                        upper_v(k, q)
                        upper_w(k, q)

        @block.vector
        def _(dve):
            v = nc.vector
            count = [0]

            def link(*several):
                for ins in several:
                    ins.then_inc(s["dchain"], 1)
                    count[0] += 1
                dve.wait_ge(s["dchain"], count[0])

            dve.wait_ge(s["par_in"], 16)
            for c in range(DC):
                dve.wait_ge(s["xT_in0" if c < 2 else "xT_in1"], 16)
                v.tensor_scalar(xg[:, c, :], xT[:, c, :], g1p[:, c:c + 1], None, ALU.mult).then_inc(s["xg_ready"], 1)
            for c in range(DC):
                dve.wait_ge(s["xhi_ready"], c + 1)
                v.tensor_tensor(xlo[:, c, :], xg[:, c, :], xhi[:, c, :].bitcast(F32), ALU.subtract).then_inc(s["xlo_ready"], 1)
            dve.wait_ge(s["consts"], 1)
            freed(dve, "ssqx")
            for i in range(CC):
                full(dve, f"xbc{i}")
                free(v.tensor_tensor(cin[:, i, CONV - 1:], bank(f"xbc{i}"), rsB[:], ALU.mult), f"xbc{i}")
                freed(dve, f"xbc{i}")
                w = [convw[:, CONV * i + j:CONV * i + j + 1] for j in range(CONV)]
                link(v.tensor_scalar(xcT[:, i, :], cin[:, i, 0:T], w[0], convb[:, i:i + 1], ALU.mult, ALU.add))
                for j in range(1, CONV):
                    ins = v.scalar_tensor_tensor(xcT[:, i, :], cin[:, i, j:j + T], w[j], xcT[:, i, :], ALU.mult, ALU.add)
                    if j < CONV - 1:
                        link(ins)
                ins.then_inc(s["conv_ready"], 1)
            full(dve, "dt")
            freed(dve, "rowx")
            dve.wait_ge(s["wdt_in"], 48)
            free(v.tensor_tensor(dts[:, 0], bank("dt")[:, 0:NT * SSD_H].rearrange("p (t h) -> p t h", t=NT),
                                 rowr[:, 0:NT].unsqueeze(2).broadcast_to([P, NT, SSD_H]), ALU.mult), "dt")
            freed(dve, "dt")
            link(v.tensor_tensor(dts[:, 0], dts[:, 0], dtb[:].unsqueeze(1).broadcast_to([P, NT, SSD_H]), ALU.add))
            v.scalar_tensor_tensor(dts[:, 1], dts[:, 0], -1.0, dts[:, 0], ALU.mult, ALU.max).then_inc(s["udt"], 1)
            dve.wait_ge(s["dtp"], 2)
            link(v.scalar_tensor_tensor(dts[:, 3], dts[:, 0], 0.0, dts[:, 2], ALU.max, ALU.add))
            v.scalar_tensor_tensor(dts[:, 4], dts[:, 3], -1.0, alog[:].unsqueeze(1).broadcast_to([P, NT, SSD_H]),
                                   ALU.mult, ALU.mult).then_inc(s["adt_ready"], 1)
            for kind, dst in (("q", qT), ("k", kT), ("z", zT), ("qm", qmT)):
                for i in range(2 if kind == "qm" else 3):
                    full(dve, f"{kind}{i}")
                    free(v.tensor_tensor(dst[:, i, :], bank(f"{kind}{i}"), rsB[:], ALU.mult), f"{kind}{i}")
            link(v.tensor_tensor(gk[:], mqg, mkg, ALU.mult))
            for c in range(DC):
                dve.wait_ge(s["sqm_ready"], c + 1)
                v.tensor_scalar(memT[:, c, :], memT[:, c, :], gmp[:, c:c + 1], None, ALU.mult).then_inc(s["memg_ready"], 1)
            freed(dve, "ssqm")
            for i in range(2):
                full(dve, f"mk{i}")
                free(v.tensor_tensor(mkT[:, i, :], bank(f"mk{i}")[:, 0:M], rmB[:], ALU.mult), f"mk{i}")
            for i in range(2):
                freed(dve, f"mkss{i}")
                v.scalar_tensor_tensor(mkT[:, i, :], mkT[:, i, :], gk[:], mksq[:, i, :], ALU.mult,
                                       ALU.mult).then_inc(s["mkn_ready"], 1)

            def ssd(t):
                cols = slice(t * P, (t + 1) * P)
                full(dve, f"cb{t}")
                free(v.tensor_tensor(cbm[:], bank(f"cb{t}")[:, 0:2 * P].rearrange("p (g l) -> p g l", g=2),
                                     upto[:].unsqueeze(1).broadcast_to([P, 2, P]), ALU.mult), f"cb{t}")
                freed(dve, f"cb{t}")
                freed(dve, f"dec{t}")
                if t < NT - 1:
                    link(v.tensor_tensor(wdd[:], dts[:, 3, t, :], dec[:, t, 0:SSD_H], ALU.mult))
                    freed(dve, f"tr{t}")
                    if t:
                        full(dve, f"st{t - 1}")
                    v.tensor_tensor(xdd[:], xn[:, t, 0:SSD_W].rearrange("p (h d) -> p h d", h=SSD_H),
                                    wdd[:].unsqueeze(2).broadcast_to([P, SSD_H, HD]), ALU.mult).then_inc(s["xdd_ready"], 1)
                freed(dve, f"segB{t}")
                freed(dve, f"segA{t}")
                for h in range(SSD_H):
                    ins = v.scalar_tensor_tensor(lm[:, t, h, :], lm[:, t, h, :], dts[:, 3, t, h:h + 1],
                                                 cbm[:, h // HPG, :], ALU.mult, ALU.mult)
                ins.then_inc(s["m_ready"], 1)
                dve.wait_ge(s["m_ready"], t + 1)
                if t:
                    freed(dve, f"ea{t}")
                    v.tensor_tensor(cdec[:, t], cdec[:, t], xcT[:, 4, cols].unsqueeze(1).broadcast_to([P, HPG, P]),
                                    ALU.mult).then_inc(s["cdec_ready"], 1)
                if t < NT - 1:
                    full(dve, f"st{t}")
                    if t == 0:
                        ins = v.tensor_copy(state[:, 1], bank("st0")[:, 0:HPG * HD].rearrange("p (h d) -> p h d", h=HPG))
                    else:
                        freed(dve, f"st{t - 1}")
                        for g in range(SSD_G):
                            r_ = slice(HD * g, HD * (g + 1))
                            for i in range(HPG):
                                a = SSD_H + HPG * g + i
                                ins = v.scalar_tensor_tensor(state[r_, t + 1, i, :], state[r_, t, i, :], dec[r_, t, a:a + 1],
                                                             bank(f"st{t}")[r_, i * HD:(i + 1) * HD], ALU.mult, ALU.add)
                    free(ins, f"st{t}")

            def normalized(n):
                c, t = divmod(n, NT)
                freed(dve, f"sc{c}{t}")
                link(v.reciprocal(mstat[:, 3, n, :], mstat[:, 2, n, :]))
                for e in range(2):
                    ins = v.tensor_scalar(pr[:, n % 3, e, :], pr[:, n % 3, e, :], mstat[:, 3, n, e:e + 1], None, ALU.mult)
                ins.then_inc(s["pn_ready"], 1)

            def memory(c, t):
                n = NT * c + t
                if t < NT:
                    full(dve, f"sc{c}{t}")
                    link(v.tensor_reduce(mstat[:, 0, n, :], bank(f"sc{c}{t}").rearrange("p (e m) -> p e m", e=2), AX.X, ALU.max))
                    v.scalar_tensor_tensor(mstat[:, 1, n, :], mstat[:, 0, n, :], -1.0, rq[:, 4 * t + 2 * c:4 * t + 2 * c + 2],
                                           ALU.mult, ALU.mult).then_inc(s["smax_ready"], 1)
                if t:
                    normalized(n - 1)
                if t == NT:
                    full(dve, f"ym{c}")
                    free(v.tensor_copy(ymix[:, 6 + c, :], bank(f"ym{c}")), f"ym{c}")
            freed(dve, "qmss")
            for kind, c, t in STEPS:
                if kind == "ssd":
                    ssd(t)
                else:
                    memory(c, t)
            for i in range(SC):
                full(dve, f"y{i}")
                free(v.scalar_tensor_tensor(yg[:, i, :], xcT[:, i, :], dskip[:, i:i + 1], bank(f"y{i}"), ALU.mult, ALU.add),
                     f"y{i}")
                freed(dve, f"y{i}")
                dve.wait_ge(s["silu_ready"], i + 1)
                v.tensor_tensor(yg[:, i, :], yg[:, i, :], zT[:, i, :], ALU.mult).then_inc(s["yg_ready"], 1)
            freed(dve, "ssqy")
            for i in range(SC):
                v.scalar_tensor_tensor(ymix[:, i, :], yg[:, i, :], ssdg[:, i:i + 1], rsB[:], ALU.mult,
                                       ALU.mult).then_inc(s["ymix_ready"], 1)

            freed(dve, "ssqym")
            freed(dve, "ym1")
            for c in range(2):
                v.scalar_tensor_tensor(ymix[:, 6 + c, :], ymix[:, 6 + c, :], memg[:, c:c + 1], xcT[:, 4, :], ALU.mult,
                                       ALU.mult).then_inc(s["ymix_ready"], 1)

            sbk = psum[:, 3:6, :].rearrange("p b n -> p (b n)")[:, 0:SB_N]
            dve.wait_ge(s["ymix_ready"], 5)

            def not_kept(h):
                dve.wait_ge(s["zs_ready"], h + 1)
                dve.wait_ge(s["lk_ready"], h + 1)
                if h >= 2:
                    dve.wait_ge(s["kept_full"], h - 1)
                v.scalar_tensor_tensor(nk[:, h % 2, :], zs[:, h % 2, :], 0.0, lk[:, h % 2, :], ALU.max,
                                       ALU.add).then_inc(s["nk_ready"], 1)

            def head_pair(c):
                dve.wait_ge(s["av_full"], 2 * c + 2)
                v.tensor_copy(ysb[:, c, :], psum[:, 6 + c % 2, :]).then_inc(s["ysb_ready"], 1)
            not_kept(0)
            for h in range(SB_H):
                if h < SB_H - 1:
                    not_kept(h + 1)
                dve.wait_ge(s["kept_full"], h + 1)
                if h >= 2:
                    dve.wait_ge(s["av_full"], h - 1)
                v.tensor_tensor(wt[:, h % 2, :], zs[:, h % 2, :], sbk, ALU.subtract).then_inc(s["arg_ready"], 1)
                if h in (3, 5):
                    head_pair(h // 2 - 1)
            head_pair(2)
            dve.wait_ge(s["rbB_ready"], 1)
            for i in range(SC):
                v.scalar_tensor_tensor(ymix[:, 3 + i, :], ysb[:, i, :], sbg[:, i:i + 1], rbB[:], ALU.mult,
                                       ALU.mult).then_inc(s["ymix_ready"], 1)

            dve.wait_ge(s["x_in"], 16)
            dve.wait_ge(s["g2_in"], 16)
            for t in range(NT + 1):
                if t < NT:
                    for half in range(2):
                        n = 2 * t + half
                        dve.wait_ge(s["o_full"], n + 1)
                        cols = slice(half * 512, (half + 1) * 512)
                        v.tensor_tensor(x1[:, t, cols], psum[:, 1 + n % 4, :], x1[:, t, cols], ALU.add).then_inc(s["x1_ready"], 1)
                if t:
                    dve.wait_ge(s["r2_ready"], t)
                    v.scalar_tensor_tensor(h2row[:, min(t - 1, 1), :], x1[:, t - 1, :], rowr2[:, t - 1:t], g2row[:], ALU.mult,
                                           ALU.mult).then_inc(s["h2row_ready"], 1)

            dotted = [0]

            def dot(j, k, turn):
                dve.wait_ge(row_in[k], 16 * turn)
                v.scalar_tensor_tensor(urow[k], urow[k], 1.0, h2row[:, 0, :], ALU.mult, ALU.mult,
                                       accum_out=dots[:, bass.ds(j, 1)]).then_inc(s["dot_ready"], 1)

            def some_dots(t, part, of):
                if t:
                    start = max(R_GATHER[t] - LAG, 0)
                    early = 4 * (R_SOFTMAX[t] - R[t][0]) - 2
                    late = H_GATHER[t - 1] - LAG - start - early
                    goal = early * part // of if part <= of else early + late * (part - of) // of
                    while dotted[0] < start + goal:
                        dot(dotted[0], dotted[0] % 4, dotted[0] // 4 + 1)
                        dotted[0] += 1

            def top16(pairs):
                link(*[v.max(val[:, 0:8], row) for row, val, at in pairs])
                link(*[v.max_index(at[:, 0:8], val[:, 0:8], row) for row, val, at in pairs])
                link(*[v.match_replace(row, val[:, 0:8], row, NEG) for row, val, at in pairs])
                link(*[v.max(val[:, 8:16], row) for row, val, at in pairs])
                link(*[v.max_index(at[:, 8:16], val[:, 8:16], row) for row, val, at in pairs])

            def route(t):
                for i in range(PH // 2):
                    dve.wait_ge(s["sco_ready"], 4 * t + i + 1)
                    top16([(sco[:, h, c, :], top[:, h, c, :], itop[:, h, c, :]) for h in (2 * i, 2 * i + 1) for c in range(2)])
                    v.tensor_copy(itopf[:, 2 * i:2 * i + 2], itop[:, 2 * i:2 * i + 2]).then_inc(s["sco_used"], 1)
                    some_dots(t, i + 1, 6)
                if t >= 2:
                    dve.wait_ge(s["g_full"], 16 * (t - 1) + 2)
                link(v.tensor_tensor(cand[:], top[:, :, 0, :].unsqueeze(3).broadcast_to([P, PH, TOPK, TOPK]),
                                     top[:, :, 1, :].unsqueeze(2).broadcast_to([P, PH, TOPK, TOPK]), ALU.add))
                for i in range(0, PH, 4):
                    top16([(cand[:, h].rearrange("p a b -> p (a b)"), best[:, h, :], pos[:, h, :]) for h in range(i, i + 4)])
                    some_dots(t, 5 + i // 4, 6)
                v.tensor_tensor(sm[:, 0], best[:], best[:, :, 0:1].broadcast_to([P, PH, TOPK]),
                                ALU.subtract).then_inc(s["soft_in"], 1)
                link(v.tensor_scalar(posab[:, 0], pos[:], 4, None, ALU.logical_shift_right),
                     v.tensor_scalar(posab[:, 1], pos[:], 15, None, ALU.bitwise_and))
                link(v.tensor_copy(posf[:], posab[:]))
                dve.wait_ge(s["sco_used"], 4 * t + 4)
                if t >= 2:
                    dve.wait_ge(s["rT_full"], t - 1)
                for c in range(2):
                    link(v.tensor_tensor(pick[:], posf[:, c].unsqueeze(3).broadcast_to([P, PH, TOPK, TOPK]),
                                         iota16[:].unsqueeze(1).unsqueeze(1).broadcast_to([P, PH, TOPK, TOPK]), ALU.is_equal))
                    link(v.tensor_tensor(pick[:], pick[:], itopf[:, :, c, :].unsqueeze(2).broadcast_to([P, PH, TOPK, TOPK]),
                                         ALU.mult))
                    link(v.tensor_reduce(routed[:, c, :].rearrange("p (h k) -> p h k", h=PH), pick[:], AX.X, ALU.add))
                    if c == 0:
                        some_dots(t, 3, 2)
                dve.wait_ge(s["soft_out"], t + 1)
                link(v.tensor_reduce(sm[:, 2, :, 0:1].rearrange("p h o -> p (h o)"), sm[:, 1], AX.X, ALU.add))
                link(v.reciprocal(sm[:, 3, :, 0:1], sm[:, 2, :, 0:1]))
                v.tensor_tensor(routed[:, 2, :].rearrange("p (h k) -> p h k", h=PH), sm[:, 1],
                                sm[:, 3, :, 0:1].broadcast_to([P, PH, TOPK]), ALU.mult).then_inc(s["routed_ready"], 1)
                if t == 0:
                    dve.wait_ge(s["routed_ready"], 1)
                    v.tensor_copy(gate0[:], routed[:, 2, :])
                    link(v.scalar_tensor_tensor(eidx[:], routed[:, 0, :], float(NK), routed[:, 1, :], ALU.mult, ALU.add))
                    dve.sem_inc(s["eidx_ready"], 1)
                some_dots(t, 4, 2)

            def hot(tt):
                a, b = H[tt]
                j0 = H_GATHER[tt] - LAG
                dve.wait_ge(s["rT_ready"], tt + 1)
                with dve.Fori(a, b) as q:
                    for n in range(8):
                        k = n % 2
                        dve.wait_ge(s["g_full"], 8 * q + (16 * tt - 8 * a + n + 1))
                        for c, hot_, ready in ((1, hotB, "hotC_ready"), (0, hotA, "hotA_ready")):
                            v.tensor_tensor(hot_[:, k], iota128[:].unsqueeze(1).broadcast_to([P, 8, P]),
                                            rT[:, c, bass.ds(64 * q + (8 * n - 64 * a), 8)].unsqueeze(2).broadcast_to([P, 8, P]),
                                            ALU.is_equal).then_inc(s[ready], 1)
                        dot(8 * q + (j0 - 8 * a + n), n % 4, 2 * q + (j0 // 4 - 2 * a + n // 4 + 1))
                dotted[0] = j0 + 8 * (b - a)
            route(0)
            for t in range(1, NT):
                route(t)
                hot(t - 1)
            v.memset(zr[:].bitcast(F32), 0.0).then_inc(s["zero_ready"], 1)
            for j in range(HK - LAG, HK):
                dot(j, j % 4, j // 4 + 1)

            dve.wait_ge(s["gate_stored"], 16 * PIECES * DT)
            dve.sem_inc(s["w_ready"], 4)
            v.memset(acc0[:], 0.0).then_inc(s["vrow_free"], 4)
            dve.wait_ge(s["ge_ready"], 1)
            link(v.tensor_tensor(wrow[:], wrow[:], gate0[:], ALU.mult))
            with dve.Fori(0, PASSES) as q:
                for k in range(4):
                    i = 4 * q + k
                    dve.wait_ge(s["vhi_ready"], i + 1)
                    v.tensor_tensor(vlo[:, k, :], vraw[:, k, :], vhi[:, k, :].bitcast(F32), ALU.subtract).then_inc(s["v_split"], 1)
                    dve.wait_ge(s["whi_ready"], i + 1)
                    v.tensor_tensor(wlo[:, k, :], wf[:, k, :], whi[:, k, :].bitcast(F32), ALU.subtract).then_inc(s["w_ready"], 1)
                    dve.wait_ge(row_in[k], 16 * q + 16 * (HK // 4 + 1))
                    dve.wait_ge(s["vrow_free"], i + 4)
                    v.scalar_tensor_tensor(acc0[:], urow[k], wrow[:, bass.ds(i, 1)], acc0[:], ALU.mult,
                                           ALU.add).then_inc(s["vrow_free"], 1)
            dve.wait_ge(s["vrow_free"], NK + 4)
            dve.wait_ge(s["x1b_in"], 16)
            v.tensor_tensor(x1b[:, 0, :], x1b[:, 0, :], acc0[:], ALU.add).then_inc(s["final_ready"], 1)
            dve.wait_ge(s["p2_done"], NK + 4)
            for t in range(1, NT):
                for half in range(2):
                    cols = slice(half * 512, (half + 1) * 512)
                    ins = v.tensor_tensor(x1b[:, t, cols], psum[:, 2 * t + half, :], x1b[:, t, cols], ALU.add)
                ins.then_inc(s["final_ready"], 1)


_NAMES = ["xT", "x", "memT", "chunks", "wdt", "par", "dtb", "alog", "g2row", "wout", "wq", "keys", "uT", "u", "v"]


def kernel(x, mem, norm1_g, w_in, conv_w, conv_b, dt_bias, a_log, d_skip, ssd_norm_g, sb_out_g, mem_norm_g,
           w_mem_kv, mq_norm_g, mk_norm_g, mem_out_g, w_out, norm2_g, peer_wq, peer_keys, peer_u, peer_v):
    import concourse.bacc as bacc
    from concourse.bass_utils import run_bass_kernel_spmd

    def blocks(a):
        return a.reshape(DC, P, -1).transpose(1, 0, 2)

    def by_channel(a):
        return a.reshape(-1, P).T

    f = lambda a: np.asarray(a)[0]
    win, wkv = f(w_in), f(w_mem_kv)
    pad = np.zeros((P, 64 - 54), np.float32)
    data = {
        "xT": blocks(f(x).T), "x": f(x), "memT": blocks(f(mem).T),
        "chunks": np.stack([blocks((wkv if kind in ("mk", "mv") else win)[:, a:a + P]) for kind, a in CHUNKS]),
        "wdt": blocks(win[:, DT_COL:DT_COL + SSD_H]),
        "par": np.concatenate([
            by_channel(f(norm1_g)), by_channel(f(mem_norm_g)),
            f(conv_w).reshape(CONV, CC, P).transpose(2, 1, 0).reshape(P, CC * CONV), by_channel(f(conv_b)),
            by_channel(np.repeat(f(d_skip), HD)), by_channel(f(ssd_norm_g)), by_channel(f(sb_out_g)),
            by_channel(f(mem_out_g)), by_channel(np.tile(f(mq_norm_g), 2)), by_channel(np.tile(f(mk_norm_g), 2)), pad], axis=1),
        "dtb": np.broadcast_to(f(dt_bias), (P, SSD_H)), "alog": np.broadcast_to(f(a_log), (P, SSD_H)),
        "g2row": np.broadcast_to(f(norm2_g), (P, D)),
        "wout": f(w_out), "wq": f(peer_wq),
        "keys": f(peer_keys).transpose(1, 3, 0, 2).reshape(P, PH, NK),
        "uT": f(peer_u).reshape(NK, P, DC, P).transpose(0, 3, 2, 1), "u": f(peer_u), "v": f(peer_v).reshape(NK, P, D),
    }
    nc = bacc.Bacc("TRN2", target_bir_lowering=False, num_devices=1)
    arrays, args = {}, []
    for name in _NAMES:
        a = np.ascontiguousarray(data[name])
        arrays[f"in_{name}"] = a
        args.append(nc.dram_tensor(f"in_{name}", a.shape, mybir.dt.from_np(a.dtype), kind="ExternalInput").ap())
    args.append(nc.dram_tensor("out_0", (T, D), F32, kind="ExternalOutput").ap())
    trunk(nc, *args)
    r = run_bass_kernel_spmd(nc, [arrays], core_ids=[0])
    return r.results[0]["out_0"].reshape(1, T, D)
```
